# Optimizing a Trainium2 kernel written in Bass

```python
import math
import jax, jax.numpy as jnp
from jax import lax
import numpy as np

D_MODEL = 2048
BATCH = 1
SEQ = 256
DEPTH = 1

N_MEM = 256
BRANCH_W = 1024
N_BRANCH = 3
CHUNK = 128
SG_GROUPS = 8
SG_GROUP_W = BRANCH_W // SG_GROUPS
SSM_GROUP_W = 16
SSM_GROUPS = BRANCH_W // SSM_GROUP_W
SSM_STATE = 64
XA_HEADS = 4
XA_HEAD_DIM = BRANCH_W // XA_HEADS
N_IN = 7 * BRANCH_W + N_BRANCH * D_MODEL
EPS = 1e-6
DT_MIN = 1e-3
DT_MAX = 1e-1
EIG_CLIP = 1e-4


def rms_norm(x, g):
    xf = x.astype(jnp.float32)
    y = xf * lax.rsqrt(jnp.mean(xf * xf, axis=-1, keepdims=True) + EPS)
    return (y * g.astype(jnp.float32)).astype(x.dtype)

def layer_norm(x, g, b):
    xf = x.astype(jnp.float32)
    mu = jnp.mean(xf, axis=-1, keepdims=True)
    xc = xf - mu
    y = xc * lax.rsqrt(jnp.mean(xc * xc, axis=-1, keepdims=True) + EPS)
    return (y * g.astype(jnp.float32) + b.astype(jnp.float32)).astype(x.dtype)

def spatial_gating(u, v, ln_g, ln_b, w_s, b_s):
    bsz, seq, _ = v.shape
    n_chunks = seq // CHUNK
    vn = layer_norm(v, ln_g, ln_b).reshape(bsz, n_chunks, CHUNK, SG_GROUPS, SG_GROUP_W)
    causal = jnp.tril(jnp.ones((CHUNK, CHUNK), dtype=bool))
    w = jnp.where(causal[None], w_s, 0).astype(vn.dtype)
    z = jnp.einsum('gts,bcsgd->bctgd', w, vn) + b_s.T[None, None, :, :, None].astype(vn.dtype)
    return u * z.reshape(bsz, seq, BRANCH_W)

def s5_branch(u, a_re, a_im, log_dt, b_re, b_im, c_re, c_im, d, glu_w, glu_b):
    bsz, seq, _ = u.shape
    f32 = jnp.float32
    uf = u.astype(f32).reshape(bsz, seq, SSM_GROUPS, SSM_GROUP_W)
    lam = lax.complex(jnp.minimum(a_re.astype(f32), -EIG_CLIP), a_im.astype(f32))
    dt = jnp.exp(log_dt.astype(f32))[:, None]
    lam_bar = jnp.exp(lam * dt)
    b_mat = lax.complex(b_re.astype(f32), b_im.astype(f32))
    b_bar = ((lam_bar - 1) / lam)[:, :, None] * b_mat
    c_mat = lax.complex(c_re.astype(f32), c_im.astype(f32))
    bu = jnp.einsum('bsgh,gph->bsgp', uf.astype(jnp.complex64), b_bar)
    a_el = jnp.broadcast_to(lam_bar, bu.shape)

    def combine(left, right):
        a_l, s_l = left
        a_r, s_r = right
        return a_r * a_l, a_r * s_l + s_r

    _, states = lax.associative_scan(combine, (a_el, bu), axis=1)
    y = jnp.einsum('bsgp,ghp->bsgh', states, c_mat).real + d.astype(f32) * uf
    y = jax.nn.gelu(y.reshape(bsz, seq, BRANCH_W)).astype(u.dtype)
    return y * jax.nn.sigmoid(y @ glu_w + glu_b)

def memory_cross_attention(q, mem_n, w_k, w_v):
    bsz, seq, _ = q.shape
    n_mem = mem_n.shape[1]
    qh = q.reshape(bsz, seq, XA_HEADS, XA_HEAD_DIM)
    k = (mem_n @ w_k).reshape(bsz, n_mem, XA_HEADS, XA_HEAD_DIM)
    v = (mem_n @ w_v).reshape(bsz, n_mem, XA_HEADS, XA_HEAD_DIM)
    scores = jnp.einsum('bshd,bmhd->bhsm', qh, k).astype(jnp.float32) * (XA_HEAD_DIM ** -0.5)
    p = jax.nn.softmax(scores, axis=-1).astype(v.dtype)
    o = jnp.einsum('bhsm,bmhd->bshd', p, v)
    return o.reshape(bsz, seq, BRANCH_W)

def hybrid_layer(x, mem, pre_g, post_g, mem_g, w_in, sg_ln_g, sg_ln_b, sg_w, sg_b,
                 a_re, a_im, log_dt, b_re, b_im, c_re, c_im, d, glu_w, glu_b,
                 xa_wk, xa_wv, w_branch, w_out):
    bsz, seq, _ = x.shape
    h = rms_norm(x, pre_g)
    proj = h @ w_in
    splits = [BRANCH_W * i for i in range(1, 8)]
    a_u, a_v, a_g, b_x, b_g, x_q, x_g, gate_logits = jnp.split(proj, splits, axis=-1)
    y_a = spatial_gating(a_u, a_v, sg_ln_g, sg_ln_b, sg_w, sg_b) * jax.nn.silu(a_g)
    y_b = s5_branch(b_x, a_re, a_im, log_dt, b_re, b_im, c_re, c_im, d, glu_w, glu_b) * jax.nn.silu(b_g)
    y_x = memory_cross_attention(x_q, rms_norm(mem, mem_g), xa_wk, xa_wv) * jax.nn.silu(x_g)
    ys = jnp.stack([y_a, y_b, y_x], axis=2)
    branch = jnp.einsum('bsnc,ncd->bsnd', ys, w_branch)
    gates = jax.nn.sigmoid(gate_logits.reshape(bsz, seq, N_BRANCH, D_MODEL))
    merged = jnp.sum(gates * branch, axis=2)
    out = merged @ w_out
    return x + rms_norm(out, post_g)

def first_inputs(seed: int = 0) -> dict:
    key = jax.random.key(seed)
    ks = jax.random.split(key, 26)
    f32 = jnp.float32

    def nrm(k, shape, scale):
        return jax.random.normal(k, shape, f32) * scale

    L, D, W = DEPTH, D_MODEL, BRANCH_W
    G, H, P = SSM_GROUPS, SSM_GROUP_W, SSM_STATE
    x = nrm(ks[0], (BATCH, SEQ, D), 1.0)
    mem = nrm(ks[1], (BATCH, N_MEM, D), 1.0)
    pre_norm_g = 1.0 + nrm(ks[2], (L, D), 0.05)
    post_norm_g = 1.0 + nrm(ks[3], (L, D), 0.05)
    mem_norm_g = 1.0 + nrm(ks[4], (L, D), 0.05)
    w_in = nrm(ks[5], (L, D, N_IN), D ** -0.5)
    sg_ln_g = 1.0 + nrm(ks[6], (L, W), 0.05)
    sg_ln_b = nrm(ks[7], (L, W), 0.01)
    sg_w = nrm(ks[8], (L, SG_GROUPS, CHUNK, CHUNK), 0.5 * CHUNK ** -0.5)
    sg_b = 1.0 + nrm(ks[9], (L, SG_GROUPS, CHUNK), 0.1)
    ssm_a_re = -0.5 + nrm(ks[10], (L, G, P), 0.01)
    ssm_a_im = jnp.broadcast_to(math.pi * jnp.arange(P, dtype=f32), (L, G, P))
    ssm_log_dt = jax.random.uniform(ks[11], (L, G), f32, math.log(DT_MIN), math.log(DT_MAX))
    ssm_b_re = nrm(ks[12], (L, G, P, H), (2 * H) ** -0.5)
    ssm_b_im = nrm(ks[13], (L, G, P, H), (2 * H) ** -0.5)
    ssm_c_re = nrm(ks[14], (L, G, H, P), P ** -0.5)
    ssm_c_im = nrm(ks[15], (L, G, H, P), P ** -0.5)
    ssm_d = nrm(ks[16], (L, G, H), 0.5)
    glu_w = nrm(ks[17], (L, W, W), W ** -0.5)
    glu_b = nrm(ks[18], (L, W), 0.01)
    xa_wk = nrm(ks[19], (L, D, W), D ** -0.5)
    xa_wv = nrm(ks[20], (L, D, W), D ** -0.5)
    w_branch = nrm(ks[21], (L, N_BRANCH, W, D), W ** -0.5)
    w_out = nrm(ks[22], (L, D, D), D ** -0.5)
    return {'x': x, 'mem': mem, 'pre_norm_g': pre_norm_g, 'post_norm_g': post_norm_g,
            'mem_norm_g': mem_norm_g, 'w_in': w_in, 'sg_ln_g': sg_ln_g, 'sg_ln_b': sg_ln_b,
            'sg_w': sg_w, 'sg_b': sg_b, 'ssm_a_re': ssm_a_re, 'ssm_a_im': ssm_a_im,
            'ssm_log_dt': ssm_log_dt, 'ssm_b_re': ssm_b_re, 'ssm_b_im': ssm_b_im,
            'ssm_c_re': ssm_c_re, 'ssm_c_im': ssm_c_im, 'ssm_d': ssm_d, 'glu_w': glu_w,
            'glu_b': glu_b, 'xa_wk': xa_wk, 'xa_wv': xa_wv, 'w_branch': w_branch, 'w_out': w_out}

def first_block(x, mem, pre_norm_g, post_norm_g, mem_norm_g, w_in, sg_ln_g, sg_ln_b, sg_w, sg_b,
              ssm_a_re, ssm_a_im, ssm_log_dt, ssm_b_re, ssm_b_im, ssm_c_re, ssm_c_im, ssm_d,
              glu_w, glu_b, xa_wk, xa_wv, w_branch, w_out):
    for l in range(DEPTH):
        x = hybrid_layer(x, mem, pre_norm_g[l], post_norm_g[l], mem_norm_g[l], w_in[l],
                         sg_ln_g[l], sg_ln_b[l], sg_w[l], sg_b[l],
                         ssm_a_re[l], ssm_a_im[l], ssm_log_dt[l], ssm_b_re[l], ssm_b_im[l],
                         ssm_c_re[l], ssm_c_im[l], ssm_d[l], glu_w[l], glu_b[l],
                         xa_wk[l], xa_wv[l], w_branch[l], w_out[l])
    return x


N_MIXERS = 2
GRID_W = 64
N_HEADS = 16
HEAD_DIM = D_MODEL // N_HEADS
WIN_H_MAX = 8
WIN_W = 16
CONV_WIDTH = 31
D_FF = 4 * D_MODEL
N_CONV_LAYERS = (DEPTH + N_MIXERS - 1) // N_MIXERS
N_NA_LAYERS = DEPTH // N_MIXERS
NORM_EPS = 1e-5


def rms_norm_2(x, g):
    xf = x.astype(jnp.float32)
    y = xf * lax.rsqrt(jnp.mean(xf * xf, axis=-1, keepdims=True) + NORM_EPS)
    return (y * g.astype(jnp.float32)).astype(x.dtype)

def layer_norm_2(x, g, b):
    xf = x.astype(jnp.float32)
    mu = jnp.mean(xf, axis=-1, keepdims=True)
    xc = xf - mu
    y = xc * lax.rsqrt(jnp.mean(xc * xc, axis=-1, keepdims=True) + NORM_EPS)
    return (y * g.astype(jnp.float32) + b.astype(jnp.float32)).astype(x.dtype)

def conformer_conv(h, w_pw1, b_pw1, w_dw, b_dw, ln_g, ln_b, w_pw2, b_pw2):
    u = h @ w_pw1 + b_pw1
    a, gate = jnp.split(u, 2, axis=-1)
    u = a * jax.nn.sigmoid(gate)
    u = lax.conv_general_dilated(
        u, w_dw[:, None, :], window_strides=(1,),
        padding=[(CONV_WIDTH // 2, CONV_WIDTH // 2)],
        dimension_numbers=("NWC", "WIO", "NWC"),
        feature_group_count=D_MODEL) + b_dw
    u = jax.nn.silu(layer_norm_2(u, ln_g, ln_b))
    return u @ w_pw2 + b_pw2

def neighbourhood_attention(h, w_qkv, b_qkv, rpb, w_o, b_o):
    bsz, t, _ = h.shape
    rows = t // GRID_W
    kh = min(WIN_H_MAX, rows)
    qkv = (h @ w_qkv + b_qkv).reshape(bsz, rows, GRID_W, 3, N_HEADS, HEAD_DIM)
    q = qkv[:, :, :, 0] * (HEAD_DIM ** -0.5)
    k = qkv[:, :, :, 1]
    v = qkv[:, :, :, 2]
    row_ids = jnp.arange(rows, dtype=jnp.int32)
    row_start = jnp.clip(row_ids - kh // 2, 0, rows - kh)
    col_ids = jnp.arange(GRID_W, dtype=jnp.int32)
    col_start = jnp.clip(col_ids - WIN_W // 2, 0, GRID_W - WIN_W)
    col_idx = col_start[:, None] + jnp.arange(WIN_W, dtype=jnp.int32)[None, :]
    col_bias_idx = col_idx - col_ids[:, None] + (WIN_W - 1)
    rpb_cols = rpb[:, :, col_bias_idx]

    def row_block(r):
        rs = row_start[r]
        q_r = lax.dynamic_index_in_dim(q, r, axis=1, keepdims=False)
        k_band = lax.dynamic_slice_in_dim(k, rs, kh, axis=1)
        v_band = lax.dynamic_slice_in_dim(v, rs, kh, axis=1)
        k_win = k_band[:, :, col_idx]
        v_win = v_band[:, :, col_idx]
        row_bias_idx = rs + jnp.arange(kh, dtype=jnp.int32) - r + (WIN_H_MAX - 1)
        bias = jnp.transpose(rpb_cols[:, row_bias_idx], (0, 2, 1, 3))
        s = jnp.einsum("bqhd,biqjhd->bhqij", q_r, k_win) + bias[None]
        p = jax.nn.softmax(
            s.astype(jnp.float32).reshape(bsz, N_HEADS, GRID_W, kh * WIN_W), axis=-1)
        p = p.reshape(s.shape).astype(v.dtype)
        return jnp.einsum("bhqij,biqjhd->bqhd", p, v_win)

    o = lax.map(row_block, row_ids)
    o = jnp.moveaxis(o, 0, 1).reshape(bsz, t, D_MODEL)
    return o @ w_o + b_o

def sq_relu_mlp(h, w_up, w_down):
    return jnp.square(jax.nn.relu(h @ w_up)) @ w_down

def second_inputs(seed: int = 0) -> dict:
    key = jax.random.key(seed)
    ks = jax.random.split(key, 24)

    def nrm(k, shape, scale):
        return jax.random.normal(k, shape, jnp.float32) * scale

    d = D_MODEL
    return {
        "x": nrm(ks[0], (BATCH, SEQ, d), 1.0),
        "norm_mix_g": 1.0 + nrm(ks[1], (DEPTH, d), 0.02),
        "norm_ffn_g": 1.0 + nrm(ks[2], (DEPTH, d), 0.02),
        "final_norm_g": 1.0 + nrm(ks[3], (d,), 0.02),
        "conv_w_pw1": nrm(ks[4], (N_CONV_LAYERS, d, 2 * d), d ** -0.5),
        "conv_b_pw1": nrm(ks[5], (N_CONV_LAYERS, 2 * d), 0.02),
        "conv_w_dw": nrm(ks[6], (N_CONV_LAYERS, CONV_WIDTH, d), CONV_WIDTH ** -0.5),
        "conv_b_dw": nrm(ks[7], (N_CONV_LAYERS, d), 0.02),
        "conv_ln_g": 1.0 + nrm(ks[8], (N_CONV_LAYERS, d), 0.02),
        "conv_ln_b": nrm(ks[9], (N_CONV_LAYERS, d), 0.02),
        "conv_w_pw2": nrm(ks[10], (N_CONV_LAYERS, d, d), d ** -0.5),
        "conv_b_pw2": nrm(ks[11], (N_CONV_LAYERS, d), 0.02),
        "na_w_qkv": nrm(ks[12], (N_NA_LAYERS, d, 3 * d), d ** -0.5),
        "na_b_qkv": nrm(ks[13], (N_NA_LAYERS, 3 * d), 0.02),
        "na_rpb": nrm(ks[14], (N_NA_LAYERS, N_HEADS, 2 * WIN_H_MAX - 1, 2 * WIN_W - 1), 0.1),
        "na_w_o": nrm(ks[15], (N_NA_LAYERS, d, d), d ** -0.5),
        "na_b_o": nrm(ks[16], (N_NA_LAYERS, d), 0.02),
        "ffn_w_up": nrm(ks[17], (DEPTH, d, D_FF), d ** -0.5),
        "ffn_w_down": nrm(ks[18], (DEPTH, D_FF, d), D_FF ** -0.5),
    }

def second_block(x, norm_mix_g, norm_ffn_g, final_norm_g,
              conv_w_pw1, conv_b_pw1, conv_w_dw, conv_b_dw, conv_ln_g, conv_ln_b,
              conv_w_pw2, conv_b_pw2,
              na_w_qkv, na_b_qkv, na_rpb, na_w_o, na_b_o,
              ffn_w_up, ffn_w_down):
    h = x
    for i in range(DEPTH):
        j = i // N_MIXERS
        hn = rms_norm_2(h, norm_mix_g[i])
        if i % N_MIXERS == 0:
            h = h + conformer_conv(hn, conv_w_pw1[j], conv_b_pw1[j], conv_w_dw[j],
                                   conv_b_dw[j], conv_ln_g[j], conv_ln_b[j],
                                   conv_w_pw2[j], conv_b_pw2[j])
        else:
            h = h + neighbourhood_attention(hn, na_w_qkv[j], na_b_qkv[j], na_rpb[j],
                                            na_w_o[j], na_b_o[j])
        h = h + sq_relu_mlp(rms_norm_2(h, norm_ffn_g[i]), ffn_w_up[i], ffn_w_down[i])
    return rms_norm_2(h, final_norm_g)


def setup_inputs(seed=0):
    out = dict(first_inputs(seed))
    for name, value in second_inputs(seed + 1).items():
        if name != "x":
            out[name + "_2"] = value
    return out


def reference(
    x, mem, pre_norm_g, post_norm_g, mem_norm_g, w_in, sg_ln_g, sg_ln_b, sg_w, sg_b, ssm_a_re,
    ssm_a_im, ssm_log_dt, ssm_b_re, ssm_b_im, ssm_c_re, ssm_c_im, ssm_d, glu_w, glu_b, xa_wk,
    xa_wv, w_branch, w_out, norm_mix_g_2, norm_ffn_g_2, final_norm_g_2, conv_w_pw1_2,
    conv_b_pw1_2, conv_w_dw_2, conv_b_dw_2, conv_ln_g_2, conv_ln_b_2, conv_w_pw2_2,
    conv_b_pw2_2, na_w_qkv_2, na_b_qkv_2, na_rpb_2, na_w_o_2, na_b_o_2, ffn_w_up_2,
    ffn_w_down_2,
):
    x = first_block(
        x, mem, pre_norm_g, post_norm_g, mem_norm_g, w_in, sg_ln_g, sg_ln_b, sg_w, sg_b,
        ssm_a_re, ssm_a_im, ssm_log_dt, ssm_b_re, ssm_b_im, ssm_c_re, ssm_c_im, ssm_d, glu_w,
        glu_b, xa_wk, xa_wv, w_branch, w_out,
    )
    return second_block(
        x, norm_mix_g_2, norm_ffn_g_2, final_norm_g_2, conv_w_pw1_2, conv_b_pw1_2, conv_w_dw_2,
        conv_b_dw_2, conv_ln_g_2, conv_ln_b_2, conv_w_pw2_2, conv_b_pw2_2, na_w_qkv_2,
        na_b_qkv_2, na_rpb_2, na_w_o_2, na_b_o_2, ffn_w_up_2, ffn_w_down_2,
    )


_drawn_inputs = setup_inputs


def setup_inputs(seed=0):
    import zlib

    import numpy as np

    out = dict(_drawn_inputs(seed))
    spreads = {}
    factors = {'mem_norm_g': 8.0,
     'sg_ln_g': 18.998,
     'sg_ln_b': 64.0,
     'ssm_a_re': 64.0,
     'ssm_a_im': 27.88,
     'ssm_log_dt': 28.112,
     'ssm_b_re': 38.296,
     'ssm_b_im': 38.296,
     'ssm_c_re': 37.992,
     'ssm_c_im': 38.536,
     'glu_w': 16.614,
     'glu_b': 64.0,
     'norm_mix_g_2': 6.061,
     'norm_ffn_g_2': 3.997,
     'final_norm_g_2': 7.809,
     'conv_b_pw1_2': 6.134,
     'conv_b_dw_2': 10.161,
     'conv_ln_g_2': 5.571,
     'conv_ln_b_2': 6.591,
     'conv_b_pw2_2': 4.078,
     'sg_b': 3.342}
    for name, (base, spread) in spreads.items():
        noise = np.random.default_rng([zlib.crc32(name.encode()), seed]).standard_normal(out[name].shape)
        drawn = base * np.exp(spread * noise) if base else spread * noise
        out[name] = __import__('jax').numpy.asarray(drawn.astype(out[name].dtype))
    for name, factor in factors.items():
        out[name] = (out[name] * factor).astype(out[name].dtype)
    return out
```

```python
import math
from contextlib import ExitStack

import numpy as np

import concourse.bass as bass
from concourse import mybir

F32 = mybir.dt.float32
F32R = mybir.dt.float32r
I32 = mybir.dt.int32
ALU = mybir.AluOpType
ACT = mybir.ActivationFunctionType
AX = mybir.AxisListType.X

T = 256
KB = 256
RAW, WN = 5, 3
CH = 1024
MAGIC = 12582912.0

C_OFF = {}
_n = 0
for _name, _w in (("pre", 16), ("memg", 16), ("post", 16), ("glub", 8), ("d", 8), ("mix", 16), ("ffn", 16),
                  ("fin", 16), ("bpw1", 32), ("bdw", 16), ("lng", 16), ("lnb", 16), ("bpw2", 16),
                  ("wdw", 496), ("are", 32), ("aim", 32), ("ldt", 32), ("iota", 16)):
    C_OFF[_name] = (_n, _w)
    _n += _w
NCONST = _n


class Queue:

    def __init__(self, name, sem):
        self.name, self.sem, self.n, self.ops = name, sem, 0, []

    def do(self, fn, *waits):
        self.n += 1
        self.ops.append((waits, fn, (self.sem, 1)))
        return (self.sem, self.n)

    def dma(self, fn, sem, value, *waits):
        self.ops.append((waits, fn, (sem, 16)))
        return (sem, value)

    def only_wait(self, *waits):
        self.ops.append((waits, None, None))

    def emit(self, eng):
        seen = {}

        def need(tok):
            sem, v = tok
            if seen.get(id(sem), 0) < v:
                eng.wait_ge(sem, v)
                seen[id(sem)] = v

        for waits, fn, inc in self.ops:
            for w in flat(waits):
                need(w)
            if fn is not None:
                fn(eng, need).then_inc(*inc)


def flat(x):
    if x is None:
        return
    if isinstance(x, list) or (isinstance(x, tuple) and (not x or isinstance(x[0], (tuple, list)) or x[0] is None)):
        for y in x:
            yield from flat(y)
    else:
        yield x


class Slots:

    def __init__(self, aps):
        self.aps, self.free, self.i = aps, [[] for _ in aps], -1

    def next(self):
        self.i = (self.i + 1) % len(self.aps)
        return self.i, self.aps[self.i], self.free[self.i]


class Pair:

    def __init__(self, hi, lo, n):
        self.hi, self.lo, self.tok = hi, lo, [None] * n


def hybrid(nc, a, out):
    with ExitStack() as ctx:
        _build(nc, a, out, ctx)


def _build(nc, a, out, ctx):
    def sem(name):
        return ctx.enter_context(nc.semaphore(name))

    ctx.enter_context(nc.sbuf_tensor("arena", [128, 212800 // 4], F32))
    base = 16512

    def at(name, off, n, dt=F32):
        return nc.alloc_sbuf_tensor_at(name, [128, n], dt, offset=base + off)[:, :]

    K1 = 1024
    o_raw, o_wh, o_wl = 0, RAW * 4 * K1, (RAW + WN) * 4 * K1
    o_H = (RAW + 2 * WN) * 4 * K1
    o_YA = o_H + 32 * K1
    o_YX = o_YA + 16 * K1
    o_YB = o_YX + 16 * K1
    o_X = o_YB + 16 * K1
    o_M = o_X + 16 * K1
    o_F = o_M + 16 * K1
    o_C = o_F + 40 * K1
    raw = at("raw", o_raw, RAW * CH).rearrange("p (s n) -> p s n", s=RAW)
    wh = at("wh", o_wh, WN * CH, F32R).rearrange("p (s n) -> p s n", s=WN)
    wl = at("wl", o_wl, WN * CH, F32R).rearrange("p (s n) -> p s n", s=WN)

    def tiles(name, off, n, dt=F32):
        return at(name, off, n * T, dt).rearrange("p (n t) -> p n t", t=T)

    Hr = tiles("Hr", o_H, 32, F32R)
    Yr = tiles("Yr", o_YA, 48, F32R)
    Xf = tiles("Xf", o_X, 16)
    Mf = tiles("Mf", o_M, 16)
    cst = at("cst", o_C, NCONST)
    o = o_C + NCONST * 4
    ones = at("ones", o, 128)
    ident = at("ident", o + 512, 128)
    small = at("small", o + 1024, 64)
    o += 1024 + 256
    nscr = 4
    assert o + nscr * 1024 <= 212800, o
    scr = Slots([at(f"scr{i}", o + i * 1024, T) for i in range(nscr)])
    Vn = at("Vn", o_F, 2048).rearrange("p (m n) -> p m n", m=2)
    uT = tiles("uT", o_F + 8 * K1, 8)
    Bs = at("Bs", o_F + 16 * K1, 2048).rearrange("p (r t n) -> p r t n", r=2, t=8)
    Cs = at("Cs", o_F + 24 * K1, 2048).rearrange("p (r k n) -> p r k n", r=2, k=32)
    tab = at("tab", o_F + 32 * K1, 2048).rearrange("p (s w k n) -> p s w k n", s=2, w=2, k=32)
    sq0 = tiles("sq0", o_YB, 16)
    ang = at("ang", o_YB, 1024)
    angt = at("angt", o_YB + 4 * K1, 1024)
    ct = at("ct", o_YB + 8 * K1, 2048).rearrange("p (r k n) -> p r k n", r=2, k=32)
    sv = at("sv", o_YA, 40 * 32).rearrange("p (i n) -> p i n", n=32)
    wcs = [at(f"wcs{i}", o_YB + 2 * i * K1, 512).rearrange("p (r t) -> p r t", r=2) for i in range(2)]
    wsc = [at(f"wsc{i}", o_YB + (4 + 2 * i) * K1, 512).rearrange("p (r t) -> p r t", r=2) for i in range(2)]
    wm1 = at("wm1", o_YB + 8 * K1, 512).rearrange("p (r t) -> p r t", r=2)
    wm2 = at("wm2", o_YB + 10 * K1, 512).rearrange("p (r t) -> p r t", r=2)
    wn1 = at("wn1", o_YB + 12 * K1, 512).rearrange("p (r t) -> p r t", r=2)
    wn2 = at("wn2", o_YB + 14 * K1, 512).rearrange("p (r t) -> p r t", r=2)
    sgw = at("sgw", o_X, 1024).rearrange("p (g t) -> p g t", g=8)
    sgb = at("sgb", o_X + 4 * K1, 1024).rearrange("p (g t) -> p g t", g=8)
    lng_b = at("lng_b", o_X + 8 * K1, 1024)
    lnb_b = at("lnb_b", o_X + 12 * K1, 1024)
    qT = tiles("qT", o_X, 8)
    KT = tiles("KT", o_X + 8 * K1, 8)
    vn = at("vn", o_M, 2048).rearrange("p (c n) -> p c n", c=2)
    zb = tiles("zb", o_M + 8 * K1, 8)
    Pb = [at(f"Pb{i}", o_M + i * K1, T) for i in range(2)]
    pT = at("pT", o_M + 2 * K1, 512).rearrange("p (m t) -> p m t", m=2)
    F0 = tiles("F0", o_F, 16)
    upad = [at(f"upad{i}", o_F + i * 1152, 286) for i in range(4)]
    keep = [at(f"keep{i}", o_F + 16 * K1 + i * K1, T) for i in range(4)]
    scr2 = Slots([at(f"scrB{i}", o_F + 20 * K1 + i * K1, T) for i in range(8)])

    bank = [ctx.enter_context(nc.psum_tensor(f"bank{i}", [128, 512], F32))[:, :] for i in range(8)]
    bfree = [[] for _ in range(8)]

    pe = Queue("pe", sem("s_pe"))
    act = Queue("act", sem("s_act"))
    dve = Queue("dve", sem("s_dve"))
    pool = Queue("pool", sem("s_pool"))
    sp = Queue("sp", sem("s_sp"))
    s_raw = [sem(f"s_raw{i}") for i in range(RAW)]

    def load(q, name, pairs, *waits):
        s = sem("s_" + name)
        for dst, src in pairs:
            tok = q.dma(lambda e, n, dst=dst, src=src: e.dma_start(dst, src), s, 16 * len(pairs), *waits)
        return tok

    def cv(name, i=0):
        off = C_OFF[name][0] + i
        return cst[:, off:off + 1]

    def cvs(name):
        off, w = C_OFF[name]
        return cst[:, off:off + w]

    def A(dst, src, func, *w, **kw):
        return act.do(lambda e, n: e.activation(dst, src, func, **kw), *w)

    def TT(dst, x, y, op, *w, q=None):
        return (q or dve).do(lambda e, n: e.tensor_tensor(dst, x, y, op), *w)

    def TS(dst, x, s1, s2, op0, op1, *w):
        if s2 is None:
            return dve.do(lambda e, n: e.tensor_scalar(dst, x, s1, None, op0), *w)
        return dve.do(lambda e, n: e.tensor_scalar(dst, x, s1, s2, op0, op1), *w)

    def STT(dst, x, s, y, op0, op1, *w):
        return dve.do(lambda e, n: e.scalar_tensor_tensor(dst, x, s, y, op0, op1), *w)

    def split(src, pair, t0, nt, waits, scale=None):
        hi, lo = pair.hi[:, t0:t0 + nt, :], pair.lo[:, t0:t0 + nt, :]
        kw = {} if scale is None else {"scale": scale}
        ta = A(hi, src, ACT.Copy, waits, **kw)
        if scale is None:
            td = TT(lo, src, hi.bitcast(F32), ALU.subtract, ta)
        else:
            td = STT(lo, src, scale, hi.bitcast(F32), ALU.mult, ALU.subtract, ta)
        for t in range(t0, t0 + nt):
            pair.tok[t] = [ta, td]
        return [ta, td]

    chunks = []
    jobs = []

    def job(kind, w, idx, nch, acts, then):
        jobs.append((kind, nch, acts, then))
        for c in range(nch):
            chunks.append(w[idx, c, :, :])

    split_tok = {}
    pe_tok = {}
    dma_tok = {}
    state = {"split": 0, "dma": 0}

    def dma_chunk():
        c = state["dma"]
        if c >= len(chunks):
            return
        s = c % RAW
        waits = [] if c < RAW else split_tok[c - RAW]
        dma_tok[c] = sp.dma(lambda e, n, c=c, s=s: e.dma_start(raw[:, s, :], chunks[c]),
                            s_raw[s], 16 * (c // RAW + 1), waits)
        state["dma"] += 1

    def split_chunk():
        c = state["split"]
        if c >= len(chunks):
            return
        r, s = c % RAW, c % WN
        free = pe_tok[c - WN] if c >= WN else None
        ta = A(wh[:, s, :], raw[:, r, :], ACT.Copy, dma_tok[c], free)
        td = TT(wl[:, s, :], raw[:, r, :], wh[:, s, :].bitcast(F32), ALU.subtract, dma_tok[c], ta)
        split_tok[c] = [ta, td]
        state["split"] += 1
        dma_chunk()

    def mm_tile(e, need, s, k0, pr, dst, first, last):
        for kk in range(8):
            k = k0 + kk
            for t in flat(pr.tok[k]):
                need(t)
            lh = wh[:, s, kk * 128:kk * 128 + 128]
            ll = wl[:, s, kk * 128:kk * 128 + 128]
            e.matmul(dst, lh, pr.hi[:, k, :], start=first and kk == 0, stop=False)
            e.matmul(dst, lh, pr.lo[:, k, :], start=False, stop=False)
            ins = e.matmul(dst, ll, pr.hi[:, k, :], start=False, stop=last and kk == 7)
        return ins

    def mm_rows(e, need, s, k0, pr, dsts, first, last):
        for kk in range(2):
            k = k0 + kk
            for t in flat(pr.tok[k]):
                need(t)
            rh = wh[:, s, kk * 512:kk * 512 + 512]
            rl = wl[:, s, kk * 512:kk * 512 + 512]
            for h in range(2):
                xh = pr.hi[:, k, h * 128:h * 128 + 128]
                xl = pr.lo[:, k, h * 128:h * 128 + 128]
                e.matmul(dsts[h], xh, rh, start=first and kk == 0, stop=False)
                e.matmul(dsts[h], xh, rl, start=False, stop=False)
                ins = e.matmul(dsts[h], xl, rh, start=False, stop=last and kk == 1)
        return ins

    background = []

    def step():
        for g in list(background):
            try:
                next(g)
            except StopIteration:
                background.remove(g)

    def drain():
        while background:
            step()

    def run_jobs():
        c = 0
        b = 0
        for kind, nch, acts, then in jobs:
            if kind == "call":
                then()
                continue
            if kind == "T":
                bs = [b % 4]
                b += 1
            else:
                bs = [b % 4, (b + 1) % 4]
                b += 2
            for i in range(nch):
                while state["split"] < min(c + WN, len(chunks)):
                    split_chunk()
                s = c % WN
                first, last = i == 0, i == nch - 1
                waits = [split_tok[c]] + ([bfree[x] for x in bs] if first else [])
                if kind == "T":
                    dst = bank[bs[0]][:, 0:T]
                    pe_tok[c] = pe.do(lambda e, n, s=s, k0=8 * i, acts=acts, dst=dst, f=first, l=last:
                                      mm_tile(e, n, s, k0, acts, dst, f, l), *waits)
                else:
                    dsts = [bank[x] for x in bs]
                    pe_tok[c] = pe.do(lambda e, n, s=s, k0=2 * i, acts=acts, dsts=dsts, f=first, l=last:
                                      mm_rows(e, n, s, k0, acts, dsts, f, l), *waits)
                c += 1
                if not last:
                    step()
            if c < len(chunks) and state["split"] <= c + WN - 1:
                split_chunk()
            done = pe_tok[c - 1]
            if kind == "T":
                bfree[bs[0]] = then(bank[bs[0]][:, 0:T], done)
            else:
                for x, f in zip(bs, then([bank[x] for x in bs], done)):
                    bfree[x] = f
            step()

    for i in range(4):
        pass
    t_x = [load(act if i % 2 else sp, f"x{i}", [(Xf[:, 4 * i:4 * i + 4, :], a["xT"][:, 4 * i:4 * i + 4, :])]) for i in range(4)]
    t_c = load(act, "cst", [(cst, a["cst"])])
    t_mem = load(act, "mem", [(Mf[:, :, :], a["memT"])])
    t_BC = load(act, "bc", [(Bs[:, :, :, :], a["BT"]), (Cs[:, :, :, :], a["CT"])])

    t_ones = dve.do(lambda e, n: e.memset(ones, 1.0 / 2048))
    t_i0 = pool.do(lambda e, n: e.memset(ident, 0.0))
    t_id = pool.do(lambda e, n: e.affine_select(out=ident, in_=ident, compare_op=ALU.not_equal, fill=1.0, base=0,
                                                pattern=[[-1, 128]], channel_multiplier=1), t_i0)

    def tree(buf, n, w):
        tok = w
        while n > 1:
            n //= 2
            tok = TT(buf[:, 0:n, :], buf[:, 0:n, :], buf[:, n:2 * n, :], ALU.add, tok)
        return tok

    def mean_of(src, w, bk=7):
        return pe.do(lambda e, n: e.matmul(bank[bk][:, 0:T], ones, src, start=True, stop=True), w, t_ones, bfree[bk])

    def rstd_of(src, dst, eps, w, wd, bk=7):
        tm = mean_of(src, w, bk)
        te = TS(dst, bank[bk][:, 0:T], eps, None, ALU.add, None, tm, wd)
        bfree[bk] = [te]
        ts_ = A(dst, dst, ACT.Sqrt, te)
        return dve.do(lambda e, n: e.reciprocal(dst, dst), ts_)

    hp = Pair(Hr[:, 0:16, :], Hr[:, 16:32, :], 16)
    mp = Pair(Yr[:, 0:16, :], Yr[:, 16:32, :], 16)

    for _ in range(RAW):
        dma_chunk_later = True

    def norm_in(buf, loads, gname, pair, sqbuf, eps, sqfree, war=None):
        ts_ = []
        for i in range(4):
            ts_.append(A(sqbuf[:, 4 * i:4 * i + 4, :], buf[:, 4 * i:4 * i + 4, :], ACT.Square, loads[i], sqfree))
        tt = tree(sqbuf, 16, ts_)
        yield
        si, rs, fr = scr.next()
        tr = rstd_of(sqbuf[:, 0, :], rs, eps, tt, fr)
        yield
        for i in range(4):
            tk = [STT(buf[:, t, :], buf[:, t, :], cv(gname, t), rs, ALU.mult, ALU.mult, tr, t_c)
                  for t in range(4 * i, 4 * i + 4)]
            yield
            split(buf[:, 4 * i:4 * i + 4, :], pair, 4 * i, 4, [tk, war])
            yield
        scr.free[si] = tk
        state["normed"] = [tk, pair.tok[15]]

    TWO_PI = 2 * math.pi
    c1 = 6.28125
    c2 = float(np.float32(math.floor((TWO_PI - c1) * 2 ** 20) / 2 ** 20))
    c3 = float(np.float32(TWO_PI - c1 - c2))

    def reduce_angle(x, t, w):
        k = TS(t, x, 1 / TWO_PI, MAGIC, ALU.mult, ALU.add, w)
        k = TS(t, t, -MAGIC, None, ALU.add, None, k)
        for c in (c1, c2, c3):
            k = STT(x, t, -c, x, ALU.mult, ALU.add, k)
        return k

    def vexp(dst, x, t1, t2, w):
        k = TS(x, x, 88.7, -103.9, ALU.min, ALU.max, w)
        k = TS(t1, x, 1 / math.log(2), MAGIC, ALU.mult, ALU.add, k)
        k = TS(t1, t1, -MAGIC, None, ALU.add, None, k)
        k = STT(x, t1, -0.693359375, x, ALU.mult, ALU.add, k)
        k = STT(x, t1, 2.12194440e-4, x, ALU.mult, ALU.add, k)
        k = TS(dst, x, 1 / 5040, None, ALU.mult, None, k)
        for c in (1 / 720, 1 / 120, 1 / 24, 1 / 6, 0.5, 1.0):
            k = STT(dst, dst, c, x, ALU.add, ALU.mult, k)
        k = TS(dst, dst, 1.0, None, ALU.add, None, k)
        k = TS(t2, t1, 0.5, MAGIC, ALU.mult, ALU.add, k)
        k = TS(t2, t2, -MAGIC, None, ALU.add, None, k)
        k = TT(t1, t1, t2, ALU.subtract, k)
        for t in (t1, t2):
            k = TS(x.bitcast(I32), t, 127.0, 8388608.0, ALU.add, ALU.mult, k)
            k = TT(dst, dst, x, ALU.mult, k)
        return k

    V = lambda i: sv[:, i, :]
    s5 = {}

    def s5_setup():
        w = state["normed"]
        k = TS(V(0), cvs("ldt"), 1.0, None, ALU.mult, None, w, t_c)
        k = vexp(V(1), V(0), V(2), V(3), k)
        yield
        k = TS(V(4), cvs("are"), -1e-4, None, ALU.min, None, k)
        k = TT(V(5), V(4), V(1), ALU.mult, k)
        k = TT(V(6), cvs("aim"), V(1), ALU.mult, k)
        k = vexp(V(7), V(5), V(2), V(3), k)
        yield
        k = reduce_angle(V(6), V(2), k)
        k = TS(V(8), V(6), 16.0, None, ALU.mult, None, k)
        k = reduce_angle(V(8), V(2), k)
        yield
        an = ang.rearrange("p (s k n) -> p s k n", s=2, k=32)
        io = cvs("iota")[:, None, :].broadcast_to((128, 32, 16))
        k1 = TT(an[:, 0, :, :], V(8)[:, :, None].broadcast_to((128, 32, 16)), io, ALU.mult, k)
        k = TT(an[:, 1, :, :], V(6)[:, :, None].broadcast_to((128, 32, 16)), io, ALU.mult, k)
        k = reduce_angle(ang, angt, [k, k1])
        yield
        k = TS(ang, ang, 3.1415925, -3.1415925, ALU.min, ALU.max, k)
        ks = A(tab[:, :, 1, :, :], an, ACT.Sin, k)
        k = STT(angt, ang, -1.0, ang, ALU.mult, ALU.min, k)
        k = TS(angt, angt, math.pi / 2, None, ALU.add, None, k)
        kc = A(tab[:, :, 0, :, :], angt.rearrange("p (s k n) -> p s k n", s=2, k=32), ACT.Sin, k)
        yield
        lbr, lbi, lr, li = V(9), V(10), V(4), cvs("aim")
        k1 = TT(lbr, V(7), tab[:, 1, 0, :, 1], ALU.mult, ks, kc)
        k2 = TT(lbi, V(7), tab[:, 1, 1, :, 1], ALU.mult)
        k3 = TT(V(11), lr, lr, ALU.mult)
        k4 = TT(V(12), li, li, ALU.mult)
        k1 = TS(lbr, lbr, -1.0, None, ALU.add, None, k1)
        k3 = TT(V(11), V(11), V(12), ALU.add, k3, k4)
        k3 = dve.do(lambda e, n: e.reciprocal(V(11), V(11)), k3)
        yield
        a1 = TT(V(13), lbr, lr, ALU.mult, k1)
        a2 = TT(V(14), lbi, li, ALU.mult, k2)
        a3 = TT(V(15), lbi, lr, ALU.mult)
        a4 = TT(V(16), lbr, li, ALU.mult)
        a1 = TT(V(13), V(13), V(14), ALU.add, a1, a2)
        a3 = TT(V(15), V(15), V(16), ALU.subtract, a3, a4)
        a1 = TT(V(13), V(13), V(11), ALU.mult, a1, k3)
        a3 = TT(V(15), V(15), V(11), ALU.mult, a3)
        yield
        cr = V(13)[:, :, None].broadcast_to((128, 32, 32))
        ci = V(15)[:, :, None].broadcast_to((128, 32, 32))
        b1 = TT(ct[:, 0, :, :], Cs[:, 0, :, :], ci, ALU.mult, a3, t_BC)
        b2 = TT(Cs[:, 0, :, :], Cs[:, 0, :, :], cr, ALU.mult, a1, b1)
        b3 = TT(ct[:, 1, :, :], Cs[:, 1, :, :], ci, ALU.mult)
        yield
        b4 = TT(Cs[:, 1, :, :], Cs[:, 1, :, :], cr, ALU.mult, b3)
        b5 = TT(Cs[:, 0, :, :], Cs[:, 0, :, :], ct[:, 1, :, :], ALU.subtract, b2, b3)
        b6 = STT(Cs[:, 1, :, :], Cs[:, 1, :, :], -1.0, ct[:, 0, :, :], ALU.mult, ALU.subtract, b4, b1)
        rk = TS(rr, V(7), 1.0, None, ALU.mult, None)
        s5["ready"] = [b5, b6, ks, kc, rk]
        s5["sv"] = [b5, b6, rk]
        yield

    rr = cvs("ldt")

    u_tok = [None] * 8
    s5y = [None] * 8
    cs_free, sc_free = [None, None], [None, None]
    w_free = {"m": None, "n": None}

    def s5_main():
        for k in range(32):
            tt, q = k // 4, k % 4
            i = k % 2
            cs, sc = wcs[i], wsc[i]
            A_ = tab[:, 0, :, k, :][:, :, :, None].broadcast_to((128, 2, 16, 16))

            def outer(dst, j, *w):
                d = dst.rearrange("p r (a b) -> p r a b", a=16)
                tok = []
                for r in range(2):
                    x = tab[:, 0, r, k, :][:, :, None].broadcast_to((128, 16, 16))
                    y = tab[:, 1, j, k, :][:, None, :].broadcast_to((128, 16, 16))
                    tok.append(TT(d[:, r, :, :], x, y, ALU.mult, *w, q=pool))
                return tok

            p1 = outer(cs, 0, s5["ready"], cs_free[i])
            p2 = outer(wn2, 1, w_free["n"])
            pa = TT(cs[:, 0, :], cs[:, 0, :], wn2[:, 1, :], ALU.subtract, p1, p2, q=pool)
            pb = TT(cs[:, 1, :], cs[:, 1, :], wn2[:, 0, :], ALU.add, q=pool)
            bk = 4 + i

            def bu(e, n, tt=tt, q=q, bk=bk):
                for r in range(2):
                    ins = e.matmul(bank[bk][:, r * T:(r + 1) * T], Bs[32 * q:32 * q + 32, r, tt, :],
                                   uT[32 * q:32 * q + 32, tt, :], start=True, stop=True)
                return ins

            tb = pe.do(bu, u_tok[tt], t_BC, bfree[bk])
            yield
            cb = cs[:, 0:1, :].broadcast_to((128, 2, T))
            sb_ = cs[:, 1:2, :].broadcast_to((128, 2, T))
            bv = bank[bk].rearrange("p (r t) -> p r t", r=2)
            m1 = TT(wm1, bv, cb, ALU.mult, tb, pa, pb, w_free["m"], s5["ready"])
            m2 = TT(wm2, bv, sb_, ALU.mult)
            bfree[bk] = [m1, m2]
            yield
            v1 = TT(wm1[:, 0, :], wm1[:, 0, :], wm2[:, 1, :], ALU.add, m1, m2)
            v2 = TT(wm1[:, 1, :], wm1[:, 1, :], wm2[:, 0, :], ALU.subtract)
            rb = rr[:, k:k + 1].broadcast_to((128, T))
            sc1 = dve.do(lambda e, n, sc=sc, rb=rb: e.tensor_tensor_scan(sc[:, 0, :], rb, wm1[:, 0, :], 0.0, ALU.mult, ALU.add), v1, sc_free[i])
            sc2 = dve.do(lambda e, n, sc=sc, rb=rb: e.tensor_tensor_scan(sc[:, 1, :], rb, wm1[:, 1, :], 0.0, ALU.mult, ALU.add), v2)
            w_free["m"] = [sc1, sc2]
            yield
            n1 = TT(wn1, sc, cb, ALU.mult, sc1, sc2, w_free["n"], q=pool)
            n2 = TT(wn2, sc, sb_, ALU.mult, pb, q=pool)
            sc_free[i] = [n1, n2]
            cs_free[i] = [n1, n2]
            n3 = TT(wn1[:, 0, :], wn1[:, 0, :], wn2[:, 1, :], ALU.subtract, n1, n2, q=pool)
            n4 = TT(wn1[:, 1, :], wn1[:, 1, :], wn2[:, 0, :], ALU.add, q=pool)
            yield

            def cy(e, n, k=k, q=q):
                e.matmul(bank[6][32 * q:32 * q + 32, 0:T], Cs[:, 0, k, :], wn1[:, 0, :], start=True, stop=False)
                return e.matmul(bank[6][32 * q:32 * q + 32, 0:T], Cs[:, 1, k, :], wn1[:, 1, :], start=False, stop=True)

            ty = pe.do(cy, n3, n4, bfree[6] if q == 0 else None)
            w_free["n"] = [ty]
            if q == 3:
                s5y[tt] = STT(uT[:, tt, :], uT[:, tt, :], cv("d", tt), bank[6][:, 0:T], ALU.mult, ALU.add, ty)
                bfree[6] = [s5y[tt]]
            yield
        s5["work_done"] = [ty]

    gp = Pair(Yr[:, 0:8, :], Yr[:, 8:16, :], 8)
    ya = Pair(Yr[:, 0:8, :], Yr[:, 8:16, :], 8)
    yx = Pair(Yr[:, 16:24, :], Yr[:, 24:32, :], 8)
    yb = Pair(Yr[:, 32:40, :], Yr[:, 40:48, :], 8)

    def s5_gelu():
        for t in range(8):
            y = uT[:, t, :]
            si, s, fr = scr.next()
            k = A(s, y, ACT.Square, s5y[t], fr)
            k = TS(s, s, 0.044715, 1.0, ALU.mult, ALU.add, k)
            k = TT(s, s, y, ALU.mult, k)
            yield
            k = A(s, s, ACT.Tanh, k, scale=math.sqrt(2 / math.pi))
            k = STT(s, s, 1.0, y, ALU.add, ALU.mult, k)
            yield
            k = A(y, s, ACT.Copy, k, scale=0.5)
            scr.free[si] = [k]
            ks = split(y, gp, t, 1, [k, state["ya_done"]])
            s5y[t] = ks
            yield

    def gated(bk, done, src_tok, other, pair, t, war=None):
        si, s, fr = scr.next()
        k1 = A(s, bk, ACT.Tanh, done, fr, scale=0.5)
        k2 = STT(s, s, 1.0, bk, ALU.add, ALU.mult, k1)
        k3 = TT(s, s, other, ALU.mult, k2, src_tok)
        ks = split(s.rearrange("p (o t) -> p o t", o=1), pair, t, 1, [k3, war], scale=0.5)
        scr.free[si] = ks
        return [k2], ks

    def ev_bx(t):
        def f(bk, done):
            u_tok[t] = A(uT[:, t, :], bk, ACT.Copy, done)
            return [u_tok[t]]
        return f

    av = {}
    sums = small[:, 0:4].rearrange("p (c g) -> p c g", c=2)
    stat = small[:, 4:16]

    def ev_av(g):
        def f(bks, done):
            r = []
            for c in range(2):
                r.append([A(vn[:, c, g * 512:(g + 1) * 512], bks[c], ACT.Copy, done, state["mem_done"],
                            accum_out=sums[:, c, g:g + 1])])
            av[g] = r
            return r
        return f

    def spatial():
        def gen():
            yield
            tg = load(sp, "sg", [(sgw[:, :, :], a["sgw"]), (sgb[:, :, :], a["sgb"]),
                                 (lng_b, a["lng"]), (lnb_b, a["lnb"])], state["x_done"])
            tm = pool.do(lambda e, n: e.affine_select(out=sgw[:, :, :], in_=sgw[:, :, :], compare_op=ALU.is_ge, fill=0.0,
                                                      base=0, pattern=[[0, 8], [1, 128]], channel_multiplier=-1), tg)
            vt = []
            for c in range(2):
                st = stat[:, 4 * c:4 * c + 4]
                k = TT(st[:, 0:1], sums[:, c, 0:1], sums[:, c, 1:2], ALU.add, av[0], av[1])
                k = TS(st[:, 0:1], st[:, 0:1], -1.0 / 1024, None, ALU.mult, None, k)
                k = A(vn[:, c, :], vn[:, c, :], ACT.Identity, k, bias=st[:, 0:1])
                k2 = A(zb.rearrange("p n t -> p (n t)")[:, c * 1024:(c + 1) * 1024], vn[:, c, :], ACT.Square, k,
                       accum_out=st[:, 1:2])
                yield
                k = TS(st[:, 1:2], st[:, 1:2], 1.0 / 1024, 1e-6, ALU.mult, ALU.add, k2)
                k = A(st[:, 1:2], st[:, 1:2], ACT.Sqrt, k)
                k = dve.do(lambda e, n, st=st: e.reciprocal(st[:, 2:3], st[:, 1:2]), k)
                k = STT(vn[:, c, :], vn[:, c, :], st[:, 2:3], lng_b, ALU.mult, ALU.mult, k, tg)
                yield
                k = TT(vn[:, c, :], vn[:, c, :], lnb_b, ALU.add, k)
                vt += [k, k2]
                yield
            for g in range(8):
                bk = 4 + g % 2

                def z(e, n, g=g, bk=bk):
                    for c in range(2):
                        ins = e.matmul(bank[bk][:, c * 128:c * 128 + 128], vn[:, c, g * 128:g * 128 + 128],
                                       sgw[:, g, :], start=True, stop=True)
                    return ins

                tz = pe.do(z, vt, tm, bfree[bk])
                bb = sgb[:, g:g + 1, :].broadcast_to((128, 2, 128))
                k = TT(zb[:, g, :].rearrange("p (c t) -> p c t", c=2),
                       bank[bk][:, 0:T].rearrange("p (c t) -> p c t", c=2), bb, ALU.add, tz)
                bfree[bk] = [k]
                av["z", g] = k
                yield
            state["sg_done"] = [k, tz]
        background.append(gen())

    def ev_au(t):
        def f(bk, done):
            k = TT(zb[:, t, :], zb[:, t, :], bk, ALU.mult, done, av["z", t])
            av["zu", t] = k
            return [k]
        return f

    def ev_ag(t):
        def f(bk, done):
            r, ks = gated(bk, done, av["zu", t], zb[:, t, :], ya, t, state["kv_done"])
            state["zb_done"] = ks
            return r
        return f

    kv = {"K": [], "V": [], "q": []}

    def ev_k(t):
        def f(bk, done):
            k = A(KT[:, t, :], bk, ACT.Copy, done, state["sg_done"])
            kv["K"].append(k)
            return [k]
        return f

    def ev_v(g):
        def f(bks, done):
            r = [[A(Vn[:, m, g * 512:(g + 1) * 512], bks[m], ACT.Copy, done)] for m in range(2)]
            kv["V"] += r
            return r
        return f

    def ev_q(t):
        def f(bk, done):
            k = A(qT[:, t, :], bk, ACT.Copy, done, state["sg_done"], scale=1.0 / 16)
            kv["q"].append(k)
            return [k]
        return f

    o_tok = [None] * 8

    def attention():
        def gen():
            pt_free = None
            pb_free = [state["zb_done"], state["zb_done"]]
            for h in range(4):
                pt = []
                for s in range(2):
                    bk = 7

                    def sc(e, n, h=h, s=s):
                        for d in range(2):
                            ins = e.matmul(bank[7][:, 0:T], qT[:, 2 * h + d, s * 128:s * 128 + 128], KT[:, 2 * h + d, :],
                                           start=d == 0, stop=d == 1)
                        return ins

                    ts_ = pe.do(sc, kv["K"], kv["q"], bfree[7])
                    P = Pb[s]
                    mx = stat[:, 4 * s:4 * s + 1]
                    sm = stat[:, 4 * s + 1:4 * s + 2]
                    yield
                    k = dve.do(lambda e, n, mx=mx: e.reduce_max(mx, bank[7][:, 0:T], AX), ts_, pb_free[s])
                    k = TS(mx, mx, -1.0, None, ALU.mult, None, k)
                    k = A(P, bank[7][:, 0:T], ACT.Exp, k, bias=mx, accum_out=sm)
                    bfree[7] = [k]
                    yield
                    k = dve.do(lambda e, n, sm=sm: e.reciprocal(sm, sm), k)
                    k = TS(P, P, sm, None, ALU.mult, None, k)

                    def tr(e, n, P=P):
                        for m in range(2):
                            ins = e.transpose(bank[7][:, 256 + m * 128:256 + m * 128 + 128], P[:, m * 128:m * 128 + 128], ident)
                        return ins

                    yield
                    k = pe.do(tr, k, t_id, bfree[7])
                    pb_free[s] = [k]
                    k = A(pT[:, :, s * 128:s * 128 + 128], bank[7][:, 256:512].rearrange("p (m t) -> p m t", m=2),
                          ACT.Copy, k, pt_free)
                    bfree[7] = [k]
                    pt.append(k)
                    yield
                last = []
                for d in range(2):
                    t = 2 * h + d

                    def pv(e, n, t=t):
                        for m in range(2):
                            ins = e.matmul(bank[7][:, 0:T], Vn[:, m, t * 128:t * 128 + 128], pT[:, m, :],
                                           start=m == 0, stop=m == 1)
                        return ins

                    k = pe.do(pv, pt, kv["V"], bfree[7])
                    last.append(k)
                    k = A(qT[:, t, :], bank[7][:, 0:T], ACT.Copy, k)
                    bfree[7] = [k]
                    o_tok[t] = k
                    yield
                pt_free = last
            state["att_done"] = [last, pb_free, k]
        background.insert(0, gen())

    def wait_attention():
        while o_tok[7] is None or "att_done" not in state:
            step()

    def ev_xg(t):
        def f(bk, done):
            r, ks = gated(bk, done, o_tok[t], qT[:, t, :], yx, t)
            state["xg_done"] = ks
            return r
        return f

    gate = {}
    mg_tok = [None] * 16

    def ev_gate(t):
        def f(bk, done):
            si, s, fr = scr.next()
            gate[t] = (si, s, A(s, bk, ACT.Tanh, done, fr, scale=0.5))
            return [gate[t][2]]
        return f

    def ev_branch(t, first):
        def f(bk, done):
            si, s, k = gate[t]
            if first:
                k = STT(Mf[:, t, :], s, 1.0, bk, ALU.add, ALU.mult, k, done, state["att_done"])
                mg_tok[t] = k
                scr.free[si] = [k]
                return [k]
            k = STT(s, s, 1.0, bk, ALU.add, ALU.mult, k, done)
            k2 = TT(Mf[:, t, :], Mf[:, t, :], s, ALU.add, k, mg_tok[t])
            scr.free[si] = [k2]
            mg_tok[t] = k2
            return [k]
        return f

    mgp = Pair(Yr[:, 0:16, :], Yr[:, 16:32, :], 16)

    def ev_branch_last(t):
        def f(bk, done):
            r = ev_branch(t, False)(bk, done)
            split(Mf[:, t:t + 1, :], mgp, t, 1, [mg_tok[t], state["yx_done"], state["glu_done"]], scale=0.5)
            return r
        return f

    def ev_glu(t):
        def f(bk, done):
            si, s, fr = scr.next()
            k = TS(s, bk, cv("glub", t), 0.5, ALU.add, ALU.mult, done, fr)
            k1 = A(s, s, ACT.Tanh, k)
            k2 = STT(uT[:, t, :], s, 1.0, uT[:, t, :], ALU.add, ALU.mult, k1, s5y[t])
            scr.free[si] = [k2]
            av["glu", t] = k2
            return [k]
        return f

    def ev_bg(t):
        def f(bk, done):
            si, s, fr = scr.next()
            k1 = A(s, bk, ACT.Tanh, done, fr, scale=0.5)
            k2 = STT(s, s, 1.0, bk, ALU.add, ALU.mult, k1)
            k3 = TT(s, s, uT[:, t, :], ALU.mult, k2, av["glu", t])
            ks = split(s.rearrange("p (o t) -> p o t", o=1), yb, t, 1, [k3, s5["work_done"]], scale=0.25)
            scr.free[si] = ks
            return [k2]
        return f

    W = a
    for t in range(8):
        job("T", W["w_bx"], t, 2, hp, ev_bx(t))
    for g in range(2):
        job("M", W["w_av"], g, 8, hp, ev_av(g))
    job("call", None, None, 0, None, None) if False else None

    def call(fn):
        jobs.append(("call", 0, None, fn))

    call(spatial)

    def flush_all():
        drain()

    call(drain)
    call(lambda: background.append(s5_main()))
    for t in range(8):
        job("T", W["w_k"], t, 2, mp, ev_k(t))
    for g in range(2):
        job("M", W["w_v"], g, 8, mp, ev_v(g))

    def after_kv():
        state["kv_done"] = [(pe.sem, pe.n)]
    call(after_kv)
    for t in range(8):
        job("T", W["w_au"], t, 2, hp, ev_au(t))
        job("T", W["w_ag"], t, 2, hp, ev_ag(t))
    for t in range(8):
        job("T", W["w_q"], t, 2, hp, ev_q(t))
    call(attention)
    for t in range(16):
        job("T", W["w_g0"], t, 2, hp, ev_gate(t))
        if t == 0:
            call(wait_attention)
        job("T", W["w_b0"], t, 1, ya, ev_branch(t, True))
    def after_a():
        state["ya_done"] = [(pe.sem, pe.n)]
    call(after_a)
    for t in range(8):
        job("T", W["w_xg"], t, 2, hp, ev_xg(t))
    for t in range(16):
        job("T", W["w_g2"], t, 2, hp, ev_gate(t))
        job("T", W["w_b2"], t, 1, yx, ev_branch(t, False))
        if t == 4:
            call(lambda: (drain(), background.append(s5_gelu())))
    call(drain)

    def after_x():
        state["yx_done"] = [(pe.sem, pe.n)]
    call(after_x)
    for t in range(8):
        job("T", W["w_glu"], t, 1, gp, ev_glu(t))

    def after_glu():
        state["glu_done"] = [(pe.sem, pe.n)]
    call(after_glu)
    for t in range(8):
        job("T", W["w_bg"], t, 2, hp, ev_bg(t))
    for t in range(16):
        job("T", W["w_g1"], t, 2, hp, ev_gate(t))
        job("T", W["w_b1"], t, 1, yb, ev_branch_last(t))

    acc = {}

    def square_sum(src, w, key, q=None):
        si, s, fr = scr2.next()
        k = A(s, src, ACT.Square, w, fr)
        dst = keep[key[1]]
        if acc.get(key) is None:
            k2 = TS(dst, s, 1.0, None, ALU.mult, None, k, acc.get(("free", key[1])))
        else:
            k2 = TT(dst, dst, s, ALU.add, k, acc[key])
        acc[key] = k2
        scr2.free[si] = [k2]
        return k

    f_tok = [None] * 16

    def ev_out(t):
        def f(bk, done):
            k = A(F0[:, t, :], bk, ACT.Copy, done, av["glu", 7], state["att_done"], s5["work_done"])
            f_tok[t] = k
            k2 = square_sum(bk, [done, s5["work_done"]], ("post", 0))
            return [k, k2]
        return f

    t_x2 = []

    def reload_x():
        t_x2.append(load(sp, "xagain", [(Xf[:, :, :], a["xT"])], state["xg_done"]))
    call(reload_x)
    for t in range(16):
        job("T", W["w_out"], t, 2, mgp, ev_out(t))

    x_tok = [None] * 16
    h1 = Pair(Hr[:, 0:16, :], Hr[:, 16:32, :], 16)

    def to_h(gname, rs, tr, pair, war):
        for t in range(16):
            k = STT(Mf[:, t, :], Xf[:, t, :], cv(gname, t), rs, ALU.mult, ALU.mult, tr, x_tok[t], war)
            split(Mf[:, t:t + 1, :], pair, t, 1, [k, war])
        return pair.tok[15]

    def post():
        tr = rstd_of(keep[0], keep[1], 1e-6, acc["post", 0], None)
        war = [(pe.sem, pe.n)]
        for t in range(16):
            k = STT(F0[:, t, :], F0[:, t, :], cv("post", t), keep[1], ALU.mult, ALU.mult, tr, f_tok[t])
            f_tok[t] = k
            if t:
                x_tok[t - 1] = TT(Xf[:, t - 1, :], Xf[:, t - 1, :], F0[:, t - 1, :], ALU.add, f_tok[t - 1], t_x2)
                square_sum(Xf[:, t - 1, :], x_tok[t - 1], ("mix", 2))
        x_tok[15] = TT(Xf[:, 15, :], Xf[:, 15, :], F0[:, 15, :], ALU.add, k, t_x2)
        square_sum(Xf[:, 15, :], x_tok[15], ("mix", 2))
        tr = rstd_of(keep[2], keep[3], 1e-5, acc["mix", 2], None)
        state["h1"] = to_h("mix", keep[3], tr, h1, [war, mg_tok[15], mgp.tok])
    call(post)

    hb = small[:, 16:32]
    pads = Slots(upad)
    conv_in = {}
    c_tok = [None] * 16

    def ev_a(t):
        def f(bk, done):
            si, s, fr = scr2.next()
            conv_in[t] = (si, s, A(s, bk, ACT.Identity, done, fr, bias=cv("bpw1", t)))
            return [conv_in[t][2]]
        return f

    def ev_gt(t):
        def f(bk, done):
            if t == 0:
                state["hb"] = TS(hb, cvs("bpw1")[:, 16:32], 0.5, None, ALU.mult, None)
            si, s, fr = scr2.next()
            kt = A(s, bk, ACT.Tanh, done, fr, state["hb"], scale=0.5, bias=hb[:, t:t + 1])
            sa, sap, ka = conv_in[t]
            while t >= 4 and c_tok[t - 4] is None:
                step()
            pi, pad, pf = pads.next()
            if t < 4:
                z1 = dve.do(lambda e, n: e.memset(pad, 0.0), state["h1"], x_tok[15])
            else:
                z1 = None
            ku = STT(pad[:, 15:271], s, 1.0, sap, ALU.add, ALU.mult, kt, ka, pf, z1)
            scr2.free[si] = [ku]
            scr2.free[sa] = [ku]
            conv_in["u", t] = (pi, pad, ku)
            if t % 2:
                background.append(conv(t - 1))
            return [kt]
        return f

    def conv(t0):
        ks = [None, None]
        for j in range(31):
            for i in range(2):
                t = t0 + i
                pi, pad, ku = conv_in["u", t]
                wj = cst[:, C_OFF["wdw"][0] + t * 31 + j:C_OFF["wdw"][0] + t * 31 + j + 1]
                if j == 0:
                    ks[i] = TS(Mf[:, t, :], pad[:, j:j + T], wj, cv("bdw", t), ALU.mult, ALU.add, ku, state["h1"], state["wdw"])
                else:
                    ks[i] = STT(Mf[:, t, :], pad[:, j:j + T], wj, Mf[:, t, :], ALU.mult, ALU.add, ks[i])
            if j % 4 == 3:
                yield
        for i in range(2):
            pads.free[conv_in["u", t0 + i][0]] = [ks[i]]
            c_tok[t0 + i] = ks[i]
        yield

    def halve_w():
        state["wdw"] = TS(cvs("wdw"), cvs("wdw"), 0.5, None, ALU.mult, None, t_c)
    call(halve_w)
    for t in range(16):
        job("T", W["w_p1"], t, 2, h1, ev_a(t))
        job("T", W["w_p1"], 16 + t, 2, h1, ev_gt(t))
    call(drain)
    cp = Pair(Yr[:, 0:16, :], Yr[:, 16:32, :], 16)
    hlb = small[:, 32:48]
    hlg = small[:, 48:64]

    def ln2():
        kb = TS(hlb, cvs("lnb"), 0.5, None, ALU.mult, None)
        kg = TS(hlg, cvs("lng"), 0.5, None, ALU.mult, None)

        def msum(e, n):
            for t in range(16):
                for x in flat(c_tok[t]):
                    n(x)
                ins = e.matmul(bank[7][:, 0:T], ones, Mf[:, t, :], start=t == 0, stop=t == 15)
            return ins
        km = pe.do(msum, bfree[7])
        km = A(keep[0], bank[7][:, 0:T], ACT.Copy, km)
        bfree[7] = [km]
        kk = []
        for j in range(4):
            mb = keep[0].rearrange("p (o t) -> p o t", o=1).broadcast_to((128, 4, T))
            kk.append(TT(Mf[:, 4 * j:4 * j + 4, :], Mf[:, 4 * j:4 * j + 4, :], mb, ALU.subtract, km))
        for t in range(16):
            square_sum(Mf[:, t, :], kk[t // 4], ("ln", 2))
        tr = rstd_of(keep[2], keep[3], 1e-5, acc["ln", 2], None)
        for t in range(16):
            m = Mf[:, t, :]
            k = TT(m, m, keep[3], ALU.mult, tr)
            si, s, fr = scr2.next()
            k1 = A(s, m, ACT.Tanh, k, fr, kb, kg, scale=hlg[:, t:t + 1], bias=hlb[:, t:t + 1])
            k2 = A(m, m, ACT.Identity, k1, scale=cv("lng", t), bias=cv("lnb", t))
            k3 = STT(m, s, 1.0, m, ALU.add, ALU.mult, k1, k2)
            scr2.free[si] = [k3]
            split(Mf[:, t:t + 1, :], cp, t, 1, k3, scale=0.5)
        state["cp"] = cp.tok[15]
    call(ln2)

    def ev_p2(t):
        def f(bk, done):
            k = STT(Xf[:, t, :], bk, cv("bpw2", t), Xf[:, t, :], ALU.add, ALU.add, done, x_tok[t])
            x_tok[t] = k
            square_sum(Xf[:, t, :], k, ("ffn", 0))
            return [k]
        return f

    for t in range(16):
        job("T", W["w_p2"], t, 2, cp, ev_p2(t))
    h2 = Pair(Hr[:, 0:16, :], Hr[:, 16:32, :], 16)

    def pre_ffn():
        tr = rstd_of(keep[0], keep[1], 1e-5, acc["ffn", 0], None)
        to_h("ffn", keep[1], tr, h2, [(pe.sem, pe.n), state["cp"]])
    call(pre_ffn)

    hid = [Pair(Yr[:, 0:16, :], Yr[:, 16:32, :], 16) for _ in range(4)]

    def ev_up(q, t):
        def f(bk, done):
            si, s, fr = scr2.next()
            k = A(s, bk, ACT.Relu, done, fr)
            k2 = TT(s, s, s, ALU.mult, k)
            ks = split(s.rearrange("p (o t) -> p o t", o=1), hid[q], t, 1, [k2, state["war_hid"]])
            scr2.free[si] = ks
            return [k]
        return f

    def ev_dn(q, t):
        def f(bk, done):
            k = TT(Xf[:, t, :], Xf[:, t, :], bk, ALU.add, done, x_tok[t])
            x_tok[t] = k
            if q == 3:
                square_sum(Xf[:, t, :], k, ("fin", 2))
            return [k]
        return f

    def mark():
        state["war_hid"] = [(pe.sem, pe.n)]

    for q in range(4):
        call(mark)
        for t in range(16):
            job("T", W["w_up"], 16 * q + t, 2, h2, ev_up(q, t))
        for t in range(16):
            job("T", W["w_dn"], 16 * q + t, 2, hid[q], ev_dn(q, t))

    s_out = sem("s_out")

    def finish():
        tr = rstd_of(keep[2], keep[3], 1e-5, acc["fin", 2], None)
        for i in range(4):
            for t in range(4 * i, 4 * i + 4):
                k = STT(Xf[:, t, :], Xf[:, t, :], cv("fin", t), keep[3], ALU.mult, ALU.mult, tr, x_tok[t])
            tok = sp.dma(lambda e, n, i=i: e.dma_start(out[:, 4 * i:4 * i + 4, :], Xf[:, 4 * i:4 * i + 4, :]),
                         s_out, 16 * (i + 1), k)
        sp.only_wait(tok)
    call(finish)

    for _ in range(RAW):
        dma_chunk()
    for _ in norm_in(Xf, t_x, "pre", hp, sq0, 1e-6, None):
        pass
    state["x_done"] = state["normed"]

    def mem_gen():
        yield from s5_setup()
        for _ in norm_in(Mf, [t_mem] * 4, "memg", mp, sqm, 1e-6, s5["ready"], war=s5["sv"]):
            yield
        state["mem_done"] = state["normed"]
        s5["ready"] = [s5["ready"], state["normed"]]
    sqm = sq0
    background.append(mem_gen())
    jobs_run = False
    run_jobs_checked(run_jobs, state, background, drain, jobs)

    with nc.Block() as block:
        @block.sync
        def _(e):
            sp.emit(e)

        @block.gpsimd
        def _(e):
            pool.emit(e)

        @block.scalar
        def _(e):
            act.emit(e)

        @block.vector
        def _(e):
            dve.emit(e)

        @block.tensor
        def _(e):
            pe.emit(e)


def run_jobs_checked(run_jobs, state, background, drain, jobs):
    for n, (kind, nch, acts, then) in enumerate(jobs):
        if kind == "M":
            jobs.insert(n, ("call", 0, None, drain))
            break
    run_jobs()
    drain()


def kernel(**x):
    import concourse.bacc as bacc
    from concourse.bass_utils import run_bass_kernel_spmd

    f = np.float32

    def cols(v):
        return np.asarray(v).reshape(-1, 128).T

    def tilesT(w):
        k, n = w.shape
        return np.ascontiguousarray(w.reshape(k // 1024, 8, 128, n // 128, 128).transpose(3, 0, 2, 1, 4)
                                    .reshape(n // 128, k // 1024, 128, 1024))

    def tilesM(w):
        k, n = w.shape
        return np.ascontiguousarray(w.reshape(k // 256, 2, 128, n // 512, 512).transpose(3, 0, 2, 1, 4)
                                    .reshape(n // 512, k // 256, 128, 1024))

    def actT(v):
        return np.ascontiguousarray(v[0].reshape(256, 16, 128).transpose(2, 1, 0))

    x = {k: np.asarray(v) for k, v in x.items()}
    pg = lambda v: v.reshape(32, 2, 64).transpose(1, 2, 0).reshape(128, 32)
    ldt = np.ascontiguousarray(np.broadcast_to(x["ssm_log_dt"][0][:, None], (64, 64)))
    wdw = x["conv_w_dw_2"][0].reshape(31, 16, 128).transpose(2, 1, 0).reshape(128, 496)
    parts = {
        "pre": cols(x["pre_norm_g"][0]), "memg": cols(x["mem_norm_g"][0]), "post": cols(x["post_norm_g"][0]),
        "glub": cols(x["glu_b"][0]), "d": cols(x["ssm_d"][0]), "mix": cols(x["norm_mix_g_2"][0]),
        "ffn": cols(x["norm_ffn_g_2"][0]), "fin": cols(x["final_norm_g_2"]), "bpw1": cols(x["conv_b_pw1_2"][0]),
        "bdw": cols(x["conv_b_dw_2"][0]), "lng": cols(x["conv_ln_g_2"][0]), "lnb": cols(x["conv_ln_b_2"][0]),
        "bpw2": cols(x["conv_b_pw2_2"][0]), "wdw": wdw, "are": pg(x["ssm_a_re"][0]), "aim": pg(x["ssm_a_im"][0]),
        "ldt": pg(ldt), "iota": np.ascontiguousarray(np.broadcast_to(np.arange(16, dtype=f), (128, 16))),
    }
    cst = np.ascontiguousarray(np.concatenate([parts[k] for k in C_OFF], axis=1))
    BT = np.zeros((128, 2, 8, 128), f)
    CT = np.zeros((128, 2, 32, 32), f)
    for r, (bn, cn) in enumerate((("ssm_b_re", "ssm_c_re"), ("ssm_b_im", "ssm_c_im"))):
        b = x[bn][0].reshape(8, 4, 2, 64, 16)
        c = x[cn][0].reshape(32, 2, 16, 64)
        for g in range(2):
            for q in range(4):
                BT[32 * q + 16 * g:32 * q + 16 * g + 16, r, :, 64 * g:64 * g + 64] = b[:, q, g].transpose(2, 0, 1)
            CT[64 * g:64 * g + 64, r, :, 16 * g:16 * g + 16] = c[:, g].transpose(2, 0, 1)
    w_in = x["w_in"][0]
    seg = lambda i: w_in[:, 1024 * i:1024 * (i + 1)]
    gts = lambda i: w_in[:, 7168 + 2048 * i:7168 + 2048 * (i + 1)]
    wd = x["ffn_w_down_2"][0]
    arrays = {
        "xT": actT(x["x"]), "memT": actT(x["mem"]), "cst": cst, "BT": BT, "CT": CT,
        "sgw": np.ascontiguousarray(x["sg_w"][0].transpose(2, 0, 1)),
        "sgb": np.ascontiguousarray(np.broadcast_to(x["sg_b"][0], (128, 8, 128))),
        "lng": np.ascontiguousarray(np.broadcast_to(x["sg_ln_g"][0], (128, 1024))),
        "lnb": np.ascontiguousarray(np.broadcast_to(x["sg_ln_b"][0], (128, 1024))),
        "w_au": tilesT(seg(0)), "w_av": tilesM(seg(1)), "w_ag": tilesT(seg(2)), "w_bx": tilesT(seg(3)),
        "w_bg": tilesT(seg(4)), "w_q": tilesT(seg(5)), "w_xg": tilesT(seg(6)),
        "w_g0": tilesT(gts(0)), "w_g1": tilesT(gts(1)), "w_g2": tilesT(gts(2)),
        "w_k": tilesT(x["xa_wk"][0]), "w_v": tilesM(x["xa_wv"][0]), "w_glu": tilesT(x["glu_w"][0]),
        "w_b0": tilesT(x["w_branch"][0, 0]), "w_b1": tilesT(x["w_branch"][0, 1]), "w_b2": tilesT(x["w_branch"][0, 2]),
        "w_out": tilesT(x["w_out"][0]), "w_p1": tilesT(x["conv_w_pw1_2"][0]), "w_p2": tilesT(x["conv_w_pw2_2"][0]),
        "w_up": tilesT(x["ffn_w_up_2"][0]),
        "w_dn": np.concatenate([tilesT(wd[2048 * i:2048 * (i + 1)]) for i in range(4)]),
    }
    nc = bacc.Bacc("TRN2", target_bir_lowering=False, num_devices=1)
    aps = {k: nc.dram_tensor(f"in_{k}", v.shape, mybir.dt.from_np(v.dtype), kind="ExternalInput").ap()
           for k, v in arrays.items()}
    out = nc.dram_tensor("out_y", (128, 16, 256), F32, kind="ExternalOutput").ap()
    hybrid(nc, aps, out)
    r = run_bass_kernel_spmd(nc, [{f"in_{k}": v for k, v in arrays.items()}], core_ids=[0])
    y = r.results[0]["out_y"]
    return np.ascontiguousarray(y.transpose(2, 1, 0).reshape(1, 256, 2048))
```

```python
import math
from contextlib import ExitStack

import numpy as np

import concourse.bass as bass
from concourse import mybir

F32 = mybir.dt.float32
F32R = mybir.dt.float32r
I32 = mybir.dt.int32
ALU = mybir.AluOpType
ACT = mybir.ActivationFunctionType
AX = mybir.AxisListType.X

T = 256
KB = 256
RAW, WN = 5, 3
CH = 1024
MAGIC = 12582912.0

C_OFF = {}
_n = 0
for _name, _w in (("pre", 16), ("memg", 16), ("post", 16), ("glub", 8), ("d", 8), ("mix", 16), ("ffn", 16),
                  ("fin", 16), ("bpw1", 32), ("bdw", 16), ("lng", 16), ("lnb", 16), ("bpw2", 16),
                  ("wdw", 496), ("are", 32), ("aim", 32), ("ldt", 32), ("iota", 16)):
    C_OFF[_name] = (_n, _w)
    _n += _w
NCONST = _n


class Queue:

    def __init__(self, name, sem):
        self.name, self.sem, self.n, self.ops = name, sem, 0, []

    def do(self, fn, *waits):
        self.n += 1
        self.ops.append((waits, fn, (self.sem, 1)))
        return (self.sem, self.n)

    def dma(self, fn, sem, value, *waits):
        self.ops.append((waits, fn, (sem, 16)))
        return (sem, value)

    def plain(self, fn):
        self.ops.append(((), fn, None))

    def only_wait(self, *waits):
        self.ops.append((waits, None, None))

    def emit(self, eng):
        seen = {}

        def need(tok):
            sem, v = tok
            if seen.get(id(sem), 0) < v:
                eng.wait_ge(sem, v)
                seen[id(sem)] = v

        for waits, fn, inc in self.ops:
            for w in flat(waits):
                need(w)
            if fn is not None:
                ins = fn(eng, need)
                if inc is not None:
                    ins.then_inc(*inc)


def flat(x):
    if x is None:
        return
    if isinstance(x, list) or (isinstance(x, tuple) and (not x or isinstance(x[0], (tuple, list)) or x[0] is None)):
        for y in x:
            yield from flat(y)
    else:
        yield x


class Slots:

    def __init__(self, aps):
        self.aps, self.free, self.i = aps, [[] for _ in aps], -1

    def next(self):
        for _ in self.aps:
            self.i = (self.i + 1) % len(self.aps)
            if self.free[self.i] is not None:
                break
        free = self.free[self.i]
        assert free is not None
        self.free[self.i] = None
        return self.i, self.aps[self.i], free


class Pair:

    def __init__(self, both, n):
        self.hi, self.lo, self.tok = both[:, 0:n, :], both[:, n:2 * n, :], [None] * n
        self.both = both.rearrange("p (h n) t -> p h n t", h=2)


def hybrid(nc, a, out):
    with ExitStack() as ctx:
        _build(nc, a, out, ctx)


def _build(nc, a, out, ctx):
    def sem(name):
        return ctx.enter_context(nc.semaphore(name))

    ctx.enter_context(nc.sbuf_tensor("arena", [128, 212800 // 4], F32))
    base = 16512

    def at(name, off, n, dt=F32):
        return nc.alloc_sbuf_tensor_at(name, [128, n], dt, offset=base + off)[:, :]

    K1 = 1024
    o_raw, o_wh, o_wl = 0, RAW * 4 * K1, (RAW + WN) * 4 * K1
    o_H = (RAW + 2 * WN) * 4 * K1
    o_YA = o_H + 32 * K1
    o_YX = o_YA + 16 * K1
    o_YB = o_YX + 16 * K1
    o_X = o_YB + 16 * K1
    o_M = o_X + 16 * K1
    o_F = o_M + 16 * K1
    o_C = o_F + 40 * K1
    raw = at("raw", o_raw, RAW * CH).rearrange("p (s n) -> p s n", s=RAW)
    wh = at("wh", o_wh, WN * CH, F32R).rearrange("p (s n) -> p s n", s=WN)
    wl = at("wl", o_wl, WN * CH, F32R).rearrange("p (s n) -> p s n", s=WN)

    def tiles(name, off, n, dt=F32):
        return at(name, off, n * T, dt).rearrange("p (n t) -> p n t", t=T)

    Hr = tiles("Hr", o_H, 32, F32R)
    Yr = tiles("Yr", o_YA, 48, F32R)
    Xf = tiles("Xf", o_X, 16)
    Mf = tiles("Mf", o_M, 16)
    cst = at("cst", o_C, NCONST)
    o = o_C + NCONST * 4
    ones = at("ones", o, 128)
    ident = at("ident", o + 512, 128)
    small = at("small", o + 1024, 64)
    o += 1024 + 256
    nscr = 4
    assert o + (nscr + 2) * 1024 <= 212800, o
    scr = Slots([at(f"scr{i}", o + i * 1024, T) for i in range(nscr)])
    Vn = at("Vn", o_F, 2048).rearrange("p (m n) -> p m n", m=2)
    uT = tiles("uT", o_F + 8 * K1, 8)
    Bs = at("Bs", o_F + 16 * K1, 2048).rearrange("p (r t n) -> p r t n", r=2, t=8)
    Cs = at("Cs", o_F + 24 * K1, 2048).rearrange("p (r k n) -> p r k n", r=2, k=32)
    tab = at("tab", o_F + 32 * K1, 2048).rearrange("p (s w k n) -> p s w k n", s=2, w=2, k=32)
    sq0 = tiles("sq0", o_YB, 16)
    ang = at("ang", o_YB, 1024)
    angt = at("angt", o_YB + 4 * K1, 1024)
    ct = at("ct", o_YB + 8 * K1, 2048).rearrange("p (r k n) -> p r k n", r=2, k=32)
    sv = at("sv", o_M, 40 * 32).rearrange("p (i n) -> p i n", n=32)
    wcs = [at(f"wcs{i}", o_YB + 2 * i * K1, 512).rearrange("p (r t) -> p r t", r=2) for i in range(2)]
    wsc = at("wsc", o_YB + 4 * K1, 512).rearrange("p (r t) -> p r t", r=2)
    wpt = at("wpt", o_YB + 6 * K1, 512).rearrange("p (r t) -> p r t", r=2)
    wm1 = at("wm1", o_YB + 8 * K1, 512).rearrange("p (r t) -> p r t", r=2)
    wm2 = at("wm2", o_YB + 10 * K1, 512).rearrange("p (r t) -> p r t", r=2)
    wn1 = at("wn1", o_YB + 12 * K1, 512).rearrange("p (r t) -> p r t", r=2)
    wn2 = at("wn2", o_YB + 14 * K1, 512).rearrange("p (r t) -> p r t", r=2)
    sgw = at("sgw", o_YX, 1024).rearrange("p (g t) -> p g t", g=8)
    sgb = at("sgb", o_YX + 4 * K1, 1024).rearrange("p (g t) -> p g t", g=8)
    lng_b = at("lng_b", o_YX + 8 * K1, 1024)
    lnb_b = at("lnb_b", o_YX + 12 * K1, 1024)
    qT = tiles("qT", o_X, 8)
    KT = tiles("KT", o_X + 8 * K1, 8)
    vn = at("vn", o_M, 2048).rearrange("p (c n) -> p c n", c=2)
    zb = tiles("zb", o_M + 8 * K1, 8)
    Pb = [at(f"Pb{i}", o + (nscr + i) * 1024, T) for i in range(2)]
    pT = at("pT", o_YX, 512).rearrange("p (m t) -> p m t", m=2)
    F0 = tiles("F0", o_F, 16)
    upad = [at(f"upad{i}", o_F + 28 * K1 + i * 1152, 286) for i in range(4)]
    F1 = tiles("F1", o_F, 16)
    keep = [at(f"keep{i}", o_F + 16 * K1 + i * K1, T) for i in range(4)]
    scr2 = Slots([at(f"scrB{i}", o_F + 20 * K1 + i * K1, T) for i in range(8)])

    bank = [ctx.enter_context(nc.psum_tensor(f"bank{i}", [128, 512], F32))[:, :] for i in range(8)]
    bfree = [[] for _ in range(8)]

    pe = Queue("pe", sem("s_pe"))
    act = Queue("act", sem("s_act"))
    dve = Queue("dve", sem("s_dve"))
    pool = Queue("pool", sem("s_pool"))
    sp = Queue("sp", sem("s_sp"))
    s_raw = [sem(f"s_raw{i}") for i in range(RAW)]

    def load(q, name, pairs, *waits):
        s = sem("s_" + name)
        for dst, src in pairs:
            tok = q.dma(lambda e, n, dst=dst, src=src: e.dma_start(dst, src), s, 16 * len(pairs), *waits)
        return tok

    def cv(name, i=0):
        off = C_OFF[name][0] + i
        return cst[:, off:off + 1]

    def cvs(name):
        off, w = C_OFF[name]
        return cst[:, off:off + w]

    def A(dst, src, func, *w, **kw):
        return act.do(lambda e, n: e.activation(dst, src, func, **kw), *w)

    def TT(dst, x, y, op, *w, q=None):
        return (q or dve).do(lambda e, n: e.tensor_tensor(dst, x, y, op), *w)

    def TS(dst, x, s1, s2, op0, op1, *w):
        if s2 is None:
            return dve.do(lambda e, n: e.tensor_scalar(dst, x, s1, None, op0), *w)
        return dve.do(lambda e, n: e.tensor_scalar(dst, x, s1, s2, op0, op1), *w)

    def STT(dst, x, s, y, op0, op1, *w):
        return dve.do(lambda e, n: e.scalar_tensor_tensor(dst, x, s, y, op0, op1), *w)

    def split(src, pair, t0, nt, waits, scale=None):
        hi, lo = pair.hi[:, t0:t0 + nt, :], pair.lo[:, t0:t0 + nt, :]
        kw = {} if scale is None else {"scale": scale}
        ta = A(hi, src, ACT.Copy, waits, **kw)
        if scale is None:
            td = TT(lo, src, hi.bitcast(F32), ALU.subtract, ta)
        else:
            td = STT(lo, src, scale, hi.bitcast(F32), ALU.mult, ALU.subtract, ta)
        for t in range(t0, t0 + nt):
            pair.tok[t] = [ta, td]
        return [ta, td]

    def comb(bk, done, dst, *w, scale=None):
        kw = {} if scale is None else {"scale": scale}
        ka = A(dst, bk[:, T:2 * T], ACT.Copy, done, *w, **kw)
        if scale is None:
            kd = TT(dst, dst, bk[:, 0:T], ALU.add, ka)
        else:
            kd = STT(dst, bk[:, 0:T], scale, dst, ALU.mult, ALU.add, ka)
        return kd, [ka, kd]

    chunks = []
    jobs = []

    def job(kind, w, idx, nch, acts, then):
        jobs.append((kind, nch, acts, then))
        for c in range(nch):
            chunks.append(w[idx, c, :, :])

    split_tok = {}
    pool_chunks = set()
    pe_tok = {}
    dma_tok = {}
    state = {"split": 0, "dma": 0, "declared": False}

    def dma_chunk():
        c = state["dma"]
        if state["declared"] and c >= len(chunks):
            return
        s = c % RAW
        waits = [] if c < RAW else split_tok[c - RAW]
        dma_tok[c] = sp.dma(lambda e, n, c=c, s=s: e.dma_start(raw[:, s, :], chunks[c]),
                            s_raw[s], 16 * (c // RAW + 1), waits)
        state["dma"] += 1

    def split_chunk():
        c = state["split"]
        if c >= len(chunks):
            return
        r, s = c % RAW, c % WN
        free = pe_tok[c - WN] if c >= WN else None
        ta = A(wh[:, s, :], raw[:, r, :], ACT.Copy, dma_tok[c], free)
        on = pool if c in pool_chunks else dve
        td = TT(wl[:, s, :], raw[:, r, :], wh[:, s, :].bitcast(F32), ALU.subtract, dma_tok[c], ta, free, q=on)
        split_tok[c] = [ta, td]
        state["split"] += 1
        dma_chunk()

    def mm_tile(e, need, s, k0, pr, dst, first, last, wide):
        for kk in range(8):
            k = k0 + kk
            for t in flat(pr.tok[k]):
                need(t)
            lh = wh[:, s, kk * 128:kk * 128 + 128]
            ll = wl[:, s, kk * 128:kk * 128 + 128]
            if wide:
                e.matmul(dst.rearrange("p (h t) -> p h t", h=2), lh, pr.both[:, :, k, :], start=first and kk == 0,
                         stop=last and kk == 7, skip_group_check=True)
                ins = e.matmul(dst[:, 0:T], ll, pr.hi[:, k, :], start=False, stop=last and kk == 7,
                               skip_group_check=True)
            else:
                e.matmul(dst[:, 0:T], lh, pr.hi[:, k, :], start=first and kk == 0, stop=False)
                e.matmul(dst[:, 0:T], lh, pr.lo[:, k, :], start=False, stop=False)
                ins = e.matmul(dst[:, 0:T], ll, pr.hi[:, k, :], start=False, stop=last and kk == 7)
        return ins

    def mm_rows(e, need, s, k0, pr, dsts, first, last):
        for kk in range(2):
            k = k0 + kk
            for t in flat(pr.tok[k]):
                need(t)
            rh = wh[:, s, kk * 512:kk * 512 + 512]
            rl = wl[:, s, kk * 512:kk * 512 + 512]
            for h in range(2):
                xh = pr.hi[:, k, h * 128:h * 128 + 128]
                xl = pr.lo[:, k, h * 128:h * 128 + 128]
                e.matmul(dsts[h], xh, rh, start=first and kk == 0, stop=False)
                e.matmul(dsts[h], xh, rl, start=False, stop=False)
                ins = e.matmul(dsts[h], xl, rh, start=False, stop=last and kk == 1)
        return ins

    background = []

    def step():
        for g in list(background):
            try:
                next(g)
            except StopIteration:
                background.remove(g)

    def drain():
        while background:
            step()

    def run_jobs():
        c = 0
        b = 0
        for kind, nch, acts, then in jobs:
            if kind == "call":
                then()
                continue
            if kind != "M":
                bs = [b % 4]
                b += 1
            else:
                bs = [b % 4, (b + 1) % 4]
                b += 2
            for i in range(nch):
                while state["split"] < min(c + WN, len(chunks)):
                    split_chunk()
                s = c % WN
                first, last = i == 0, i == nch - 1
                waits = [split_tok[c]] + ([bfree[x] for x in bs] if first else [])
                if kind != "M":
                    dst = bank[bs[0]]
                    pe_tok[c] = pe.do(lambda e, n, s=s, k0=8 * i, acts=acts, dst=dst, f=first, l=last, w=kind == "W":
                                      mm_tile(e, n, s, k0, acts, dst, f, l, w), *waits)
                else:
                    dsts = [bank[x] for x in bs]
                    pe_tok[c] = pe.do(lambda e, n, s=s, k0=2 * i, acts=acts, dsts=dsts, f=first, l=last:
                                      mm_rows(e, n, s, k0, acts, dsts, f, l), *waits)
                c += 1
                if not last:
                    step()
            if c < len(chunks) and state["split"] <= c + WN - 1:
                split_chunk()
            done = pe_tok[c - 1]
            if kind == "T":
                bfree[bs[0]] = then(bank[bs[0]][:, 0:T], done)
            elif kind == "W":
                bfree[bs[0]] = then(bank[bs[0]], done)
            else:
                for x, f in zip(bs, then([bank[x] for x in bs], done)):
                    bfree[x] = f
            step()

    t_x = [load(act if i % 2 else sp, f"x{i}", [(Xf[:, 4 * i:4 * i + 4, :], a["xT"][:, 4 * i:4 * i + 4, :])]) for i in range(4)]
    t_c = load(act, "cst", [(cst, a["cst"])])
    for _ in range(RAW):
        dma_chunk()
    t_mem = load(sp, "mem", [(Mf[:, :, :], a["memT"])])
    t_BC = load(sp, "bc", [(Bs[:, :, :, :], a["BT"]), (Cs[:, :, :, :], a["CT"])])

    t_ones = dve.do(lambda e, n: e.memset(ones, 1.0 / 2048))
    t_i0 = pool.do(lambda e, n: e.memset(ident, 0.0))
    t_id = pool.do(lambda e, n: e.affine_select(out=ident, in_=ident, compare_op=ALU.not_equal, fill=1.0, base=0,
                                                pattern=[[-1, 128]], channel_multiplier=1), t_i0)

    def tree(buf, n, w):
        tok = w
        while n > 1:
            n //= 2
            tok = TT(buf[:, 0:n, :], buf[:, 0:n, :], buf[:, n:2 * n, :], ALU.add, tok)
        return tok

    def mean_of(src, w, bk=7):
        return pe.do(lambda e, n: e.matmul(bank[bk][:, 0:T], ones, src, start=True, stop=True), w, t_ones, bfree[bk])

    def rstd_of(src, dst, eps, w, wd, bk=7, tm=None):
        tm = tm or mean_of(src, w, bk)
        te = TS(dst, bank[bk][:, 0:T], eps, None, ALU.add, None, tm, wd)
        bfree[bk] = [te]
        ts_ = A(dst, dst, ACT.Sqrt, te)
        return dve.do(lambda e, n: e.reciprocal(dst, dst), ts_)

    hp = Pair(Hr, 16)
    mp = Pair(Yr[:, 0:32, :], 16)

    def norm_in(buf, loads, gname, pair, sqbuf, eps, sqfree, fast=False):
        ts_ = []
        for i in range(4):
            ts_.append(A(sqbuf[:, 4 * i:4 * i + 4, :], buf[:, 4 * i:4 * i + 4, :], ACT.Square, loads[i], sqfree))
            yield
        rs, fr = sqbuf[:, 15, :], None
        if fast:
            for _ in range(WN):
                split_chunk()

            def msum(e, n):
                for t in range(16):
                    for x in flat(ts_[t // 4]):
                        n(x)
                    ins = e.matmul(bank[7][:, 0:T], ones, sqbuf[:, t, :], start=t == 0, stop=t == 15)
                return ins
            tr = rstd_of(None, rs, eps, None, fr, tm=pe.do(msum, t_ones))
        else:
            tt = tree(sqbuf, 16, ts_)
            yield
            tr = rstd_of(sqbuf[:, 0, :], rs, eps, tt, fr)
        yield
        for i in range(4):
            for j in range(2):
                t0 = 4 * i + 2 * j
                tk = [STT(buf[:, t, :], buf[:, t, :], cv(gname, t), rs, ALU.mult, ALU.mult, tr, t_c)
                      for t in range(t0, t0 + 2)]
                split(buf[:, t0:t0 + 2, :], pair, t0, 2, tk)
                yield
        state["normed"] = [tk, pair.tok[15]]

    TWO_PI = 2 * math.pi
    c1 = 6.28125
    c2 = float(np.float32(math.floor((TWO_PI - c1) * 2 ** 20) / 2 ** 20))
    c3 = float(np.float32(TWO_PI - c1 - c2))

    def reduce_angle(x, t, w):
        k = TS(t, x, 1 / TWO_PI, MAGIC, ALU.mult, ALU.add, w)
        k = TS(t, t, -MAGIC, None, ALU.add, None, k)
        yield
        for c in (c1, c2, c3):
            k = STT(x, t, -c, x, ALU.mult, ALU.add, k)
        yield
        return k

    def vexp(dst, x, t1, t2, w):
        k = TS(x, x, 88.7, -103.9, ALU.min, ALU.max, w)
        k = TS(t1, x, 1 / math.log(2), MAGIC, ALU.mult, ALU.add, k)
        k = TS(t1, t1, -MAGIC, None, ALU.add, None, k)
        yield
        k = STT(x, t1, -0.693359375, x, ALU.mult, ALU.add, k)
        k = STT(x, t1, 2.12194440e-4, x, ALU.mult, ALU.add, k)
        k2 = TS(t2, t1, 0.5, MAGIC, ALU.mult, ALU.add)
        k = TS(dst, x, 1 / 5040, None, ALU.mult, None, k)
        k2 = TS(t2, t2, -MAGIC, None, ALU.add, None, k2)
        yield
        for i, c in enumerate((1 / 720, 1 / 120, 1 / 24, 1 / 6, 0.5, 1.0)):
            k = STT(dst, dst, c, x, ALU.add, ALU.mult, k)
            if i == 0:
                k2 = TT(t1, t1, t2, ALU.subtract, k2)
            if i == 3:
                yield
        k = TS(dst, dst, 1.0, None, ALU.add, None, k)
        yield
        for t in (t1, t2):
            k = TS(x.bitcast(I32), t, 127.0, 8388608.0, ALU.add, ALU.mult, k, k2)
            k = TT(dst, dst, x, ALU.mult, k)
        yield
        return k

    V = lambda i: sv[:, i, :]
    s5 = {}

    def s5_setup():
        w = state["normed"]
        k = TS(V(0), cvs("ldt"), 1.0, None, ALU.mult, None, w, t_c)
        k = yield from vexp(V(1), V(0), V(2), V(3), k)
        yield
        k = TS(V(4), cvs("are"), -1e-4, None, ALU.min, None, k)
        k = TT(V(5), V(4), V(1), ALU.mult, k)
        k = TT(V(6), cvs("aim"), V(1), ALU.mult, k)
        k = yield from vexp(V(7), V(5), V(2), V(3), k)
        yield
        k = yield from reduce_angle(V(6), V(2), k)
        k = TS(V(8), V(6), 16.0, None, ALU.mult, None, k)
        k = yield from reduce_angle(V(8), V(2), k)
        yield
        an = ang.rearrange("p (s k n) -> p s k n", s=2, k=32)
        io = cvs("iota")[:, None, :].broadcast_to((128, 32, 16))
        k1 = TT(an[:, 0, :, :], V(8)[:, :, None].broadcast_to((128, 32, 16)), io, ALU.mult, k)
        k = TT(an[:, 1, :, :], V(6)[:, :, None].broadcast_to((128, 32, 16)), io, ALU.mult, k)
        k = yield from reduce_angle(ang, angt, [k, k1])
        yield
        k = TS(ang, ang, 3.1415925, -3.1415925, ALU.min, ALU.max, k)
        ks = A(tab[:, :, 1, :, :], an, ACT.Sin, k)
        k = STT(angt, ang, -1.0, ang, ALU.mult, ALU.min, k)
        k = TS(angt, angt, math.pi / 2, None, ALU.add, None, k)
        kc = A(tab[:, :, 0, :, :], angt.rearrange("p (s k n) -> p s k n", s=2, k=32), ACT.Sin, k)
        yield
        lbr, lbi, lr, li = V(9), V(10), V(4), cvs("aim")
        k1 = TT(lbr, V(7), tab[:, 1, 0, :, 1], ALU.mult, ks, kc)
        k2 = TT(lbi, V(7), tab[:, 1, 1, :, 1], ALU.mult)
        k3 = TT(V(11), lr, lr, ALU.mult)
        k4 = TT(V(12), li, li, ALU.mult)
        k1 = TS(lbr, lbr, -1.0, None, ALU.add, None, k1)
        k3 = TT(V(11), V(11), V(12), ALU.add, k3, k4)
        k3 = dve.do(lambda e, n: e.reciprocal(V(11), V(11)), k3)
        yield
        a1 = TT(V(13), lbr, lr, ALU.mult, k1)
        a2 = TT(V(14), lbi, li, ALU.mult, k2)
        a3 = TT(V(15), lbi, lr, ALU.mult)
        a4 = TT(V(16), lbr, li, ALU.mult)
        a1 = TT(V(13), V(13), V(14), ALU.add, a1, a2)
        a3 = TT(V(15), V(15), V(16), ALU.subtract, a3, a4)
        a1 = TT(V(13), V(13), V(11), ALU.mult, a1, k3)
        a3 = TT(V(15), V(15), V(11), ALU.mult, a3)
        yield
        cr = V(13)[:, :, None].broadcast_to((128, 32, 32))
        ci = V(15)[:, :, None].broadcast_to((128, 32, 32))
        b1 = TT(ct[:, 0, :, :], Cs[:, 0, :, :], ci, ALU.mult, a3, t_BC)
        yield
        b2 = TT(Cs[:, 0, :, :], Cs[:, 0, :, :], cr, ALU.mult, a1, b1)
        b3 = TT(ct[:, 1, :, :], Cs[:, 1, :, :], ci, ALU.mult)
        yield
        b4 = TT(Cs[:, 1, :, :], Cs[:, 1, :, :], cr, ALU.mult, b3)
        yield
        b5 = TT(Cs[:, 0, :, :], Cs[:, 0, :, :], ct[:, 1, :, :], ALU.subtract, b2, b3)
        yield
        b6 = STT(Cs[:, 1, :, :], Cs[:, 1, :, :], -1.0, ct[:, 0, :, :], ALU.mult, ALU.subtract, b4, b1)
        rk = TS(rr, V(7), 1.0, None, ALU.mult, None)
        s5["ready"] = [b5, b6, ks, kc, rk]
        s5["sv"] = [b5, b6, rk]
        state["s5_ready"] = True
        yield

    rr = cvs("ldt")

    av = {}
    u_tok = [None] * 8
    s5y = [None] * 8
    cs_free = [None, None]
    w_free = {"m": None, "n": None, "s": None, "p": None}

    def s5_tables(k):
        i = k % 2
        cs = wcs[i]

        def outer(dst, j, *w):
            d = dst.rearrange("p r (a b) -> p r a b", a=16)
            tok = []
            for r in range(2):
                x = tab[:, 0, r, k, :][:, :, None].broadcast_to((128, 16, 16))
                y = tab[:, 1, j, k, :][:, None, :].broadcast_to((128, 16, 16))
                tok.append(TT(d[:, r, :, :], x, y, ALU.mult, *w, q=pool))
            return tok

        p1 = outer(cs, 0, s5["ready"], cs_free[i])
        p2 = outer(wpt, 1, w_free["p"])
        pa = TT(cs[:, 0, :], cs[:, 0, :], wpt[:, 1, :], ALU.subtract, p1, p2, q=pool)
        pb = TT(cs[:, 1, :], cs[:, 1, :], wpt[:, 0, :], ALU.add, q=pool)
        w_free["p"] = [pa, pb]
        return [pa, pb]

    def s5_main():
        cy = None
        tk = s5_tables(0)
        for k in range(32):
            tt, q = k // 4, k % 4
            i = k % 2
            cs, sc = wcs[i], wsc
            bk = 4 + i

            def bu(e, n, tt=tt, q=q, bk=bk):
                for r in range(2):
                    ins = e.matmul(bank[bk][:, r * T:(r + 1) * T], Bs[32 * q:32 * q + 32, r, tt, :],
                                   uT[32 * q:32 * q + 32, tt, :], start=True, stop=True)
                return ins

            tb = pe.do(bu, u_tok[tt], t_BC, bfree[bk])
            tk_now = tk
            if k < 31:
                tk = s5_tables(k + 1)
            yield
            cb = cs[:, 0:1, :].broadcast_to((128, 2, T))
            sb_ = cs[:, 1:2, :].broadcast_to((128, 2, T))
            bv = bank[bk].rearrange("p (r t) -> p r t", r=2)
            m1 = TT(wm1, bv, cb, ALU.mult, tb, tk_now, s5["ready"], w_free["m"])
            m2 = TT(wm2, bv, sb_, ALU.mult)
            bfree[bk] = [m1, m2]
            yield
            if cy:
                cy()
            v1 = TT(wm1[:, 0, :], wm1[:, 0, :], wm2[:, 1, :], ALU.add, m1, m2)
            v2 = TT(wm1[:, 1, :], wm1[:, 1, :], wm2[:, 0, :], ALU.subtract)
            rb = rr[:, k:k + 1].broadcast_to((128, T))
            sc1 = dve.do(lambda e, n, sc=sc, rb=rb: e.tensor_tensor_scan(sc[:, 0, :], rb, wm1[:, 0, :], 0.0, ALU.mult, ALU.add), v1, w_free["s"])
            sc2 = dve.do(lambda e, n, sc=sc, rb=rb: e.tensor_tensor_scan(sc[:, 1, :], rb, wm1[:, 1, :], 0.0, ALU.mult, ALU.add), v2)
            w_free["m"] = [sc1, sc2]
            yield
            n1 = TT(wn1, sc, cb, ALU.mult, sc1, sc2, w_free["n"])
            n2 = TT(wn2, sc, sb_, ALU.mult)
            w_free["s"] = [n1, n2]
            cs_free[i] = [n1, n2]
            n3 = TT(wn1[:, 0, :], wn1[:, 0, :], wn2[:, 1, :], ALU.subtract, n1, n2)
            n4 = TT(wn1[:, 1, :], wn1[:, 1, :], wn2[:, 0, :], ALU.add)
            yield

            def cy(k=k, q=q, tt=tt, n3=n3, n4=n4):
                def mm(e, n):
                    e.matmul(bank[6][32 * q:32 * q + 32, 0:T], Cs[:, 0, k, :], wn1[:, 0, :], start=True, stop=False)
                    return e.matmul(bank[6][32 * q:32 * q + 32, 0:T], Cs[:, 1, k, :], wn1[:, 1, :], start=False, stop=True)

                ty = pe.do(mm, n3, n4, bfree[6] if q == 0 else None)
                w_free["n"] = [ty]
                if q == 3:
                    s5y[tt] = STT(uT[:, tt, :], uT[:, tt, :], cv("d", tt), bank[6][:, 0:T], ALU.mult, ALU.add, ty)
                    bfree[6] = [s5y[tt]]
        cy()
        s5["work_done"] = [w_free["n"], w_free["p"], w_free["m"], w_free["s"]]

    gp = Pair(Yr[:, 0:16, :], 8)
    ya = Pair(Yr[:, 0:16, :], 8)
    yx = Pair(Yr[:, 16:32, :], 8)
    yb = Pair(Yr[:, 32:48, :], 8)

    def s5_gelu():
        while "ya_done" not in state:
            yield
        for t in range(8):
            y = uT[:, t, :]
            si, s, fr = scr.next()
            k = A(s, y, ACT.Square, s5y[t], fr)
            k = TS(s, s, 0.044715, 1.0, ALU.mult, ALU.add, k)
            k = TT(s, s, y, ALU.mult, k)
            yield
            k = A(s, s, ACT.Tanh, k, scale=math.sqrt(2 / math.pi))
            k = STT(s, s, 1.0, y, ALU.add, ALU.mult, k)
            yield
            k = A(y, s, ACT.Copy, k, scale=0.5)
            scr.free[si] = [k]
            ks = split(y, gp, t, 1, [k, state["ya_done"]])
            s5y[t] = ks
            yield

    def gated(bk, done, src_tok, other, pair, t, war=None):
        si, s, fr = scr.next()
        k0, rd = comb(bk, done, s, fr)
        k1 = A(s, s, ACT.Silu, k0)
        k3 = TT(s, s, other, ALU.mult, k1, src_tok)
        ks = split(s.rearrange("p (o t) -> p o t", o=1), pair, t, 1, [k3, war])
        scr.free[si] = ks
        return rd, ks

    def ev_bx(t):
        def f(bk, done):
            u_tok[t], rd = comb(bk, done, uT[:, t, :])
            return rd
        return f

    sums = small[:, 0:4].rearrange("p (c g) -> p c g", c=2)
    stat = small[:, 4:16]

    def ev_av(g):
        def f(bks, done):
            r = []
            for c in range(2):
                r.append([A(vn[:, c, g * 512:(g + 1) * 512], bks[c], ACT.Copy, done, s5["sv"],
                            accum_out=sums[:, c, g:g + 1])])
            av[g] = r
            return r
        return f

    def spatial():
        def gen():
            yield
            tg = load(sp, "sg", [(sgw[:, :, :], a["sgw"]), (sgb[:, :, :], a["sgb"]),
                                 (lng_b, a["lng"]), (lnb_b, a["lnb"])], state["kv_done"])
            tm = pool.do(lambda e, n: e.affine_select(out=sgw[:, :, :], in_=sgw[:, :, :], compare_op=ALU.is_ge, fill=0.0,
                                                      base=0, pattern=[[0, 8], [1, 128]], channel_multiplier=-1), tg)
            vt = []
            for c in range(2):
                st = stat[:, 4 * c:4 * c + 4]
                k = TT(st[:, 0:1], sums[:, c, 0:1], sums[:, c, 1:2], ALU.add, av[0], av[1])
                k = TS(st[:, 0:1], st[:, 0:1], -1.0 / 1024, None, ALU.mult, None, k)
                k = A(vn[:, c, :], vn[:, c, :], ACT.Identity, k, bias=st[:, 0:1])
                k2 = A(zb.rearrange("p n t -> p (n t)")[:, c * 1024:(c + 1) * 1024], vn[:, c, :], ACT.Square, k,
                       accum_out=st[:, 1:2])
                yield
                k = TS(st[:, 1:2], st[:, 1:2], 1.0 / 1024, 1e-6, ALU.mult, ALU.add, k2)
                k = A(st[:, 1:2], st[:, 1:2], ACT.Sqrt, k)
                k = dve.do(lambda e, n, st=st: e.reciprocal(st[:, 2:3], st[:, 1:2]), k)
                k = STT(vn[:, c, :], vn[:, c, :], st[:, 2:3], lng_b, ALU.mult, ALU.mult, k, tg)
                yield
                k = TT(vn[:, c, :], vn[:, c, :], lnb_b, ALU.add, k)
                vt += [k, k2]
                yield
            for g in range(8):
                bk = 7

                def z(e, n, g=g, bk=bk):
                    for c in range(2):
                        ins = e.matmul(bank[bk][:, c * 128:c * 128 + 128], vn[:, c, g * 128:g * 128 + 128],
                                       sgw[:, g, :], start=True, stop=True)
                    return ins

                tz = pe.do(z, vt, tm, bfree[bk])
                bb = sgb[:, g:g + 1, :].broadcast_to((128, 2, 128))
                k = TT(zb[:, g, :].rearrange("p (c t) -> p c t", c=2),
                       bank[bk][:, 0:T].rearrange("p (c t) -> p c t", c=2), bb, ALU.add, tz)
                bfree[bk] = [k]
                av["z", g] = k
                yield
            state["sg_done"] = [k, tz]
        background.append(gen())

    def ev_au(t):
        def f(bk, done):
            si, s, fr = scr.next()
            k, rd = comb(bk, done, s, fr)
            k = TT(zb[:, t, :], zb[:, t, :], s, ALU.mult, k, av["z", t])
            scr.free[si] = [k]
            av["zu", t] = k
            return rd
        return f

    def ev_ag(t):
        def f(bk, done):
            r, ks = gated(bk, done, av["zu", t], zb[:, t, :], ya, t, state["kv_done"])
            state["zb_done"] = ks
            return r
        return f

    kv = {"K": [], "V": [], "q": []}

    def ev_k(t):
        def f(bk, done):
            k, rd = comb(bk, done, KT[:, t, :], state["x_done"])
            kv["K"].append(k)
            return rd
        return f

    def ev_v(g):
        def f(bks, done):
            r = [[A(Vn[:, m, g * 512:(g + 1) * 512], bks[m], ACT.Copy, done)] for m in range(2)]
            kv["V"] += r
            return r
        return f

    def ev_q(t):
        def f(bk, done):
            k, rd = comb(bk, done, qT[:, t, :], state["x_done"], scale=1.0 / 16)
            kv["q"].append(k)
            return rd
        return f

    o_tok = [None] * 8

    def attention():
        def gen():
            pb_free = [None, None]
            pt_free = state["sg_done"]
            for h in range(4):
                pt = []
                for s in range(2):
                    bk = 7

                    def sc(e, n, h=h, s=s):
                        for d in range(2):
                            ins = e.matmul(bank[7][:, 0:T], qT[:, 2 * h + d, s * 128:s * 128 + 128], KT[:, 2 * h + d, :],
                                           start=d == 0, stop=d == 1)
                        return ins

                    ts_ = pe.do(sc, kv["K"], kv["q"], bfree[7])
                    P = Pb[s]
                    mx = stat[:, 4 * s:4 * s + 1]
                    sm = stat[:, 4 * s + 1:4 * s + 2]
                    yield
                    k = dve.do(lambda e, n, mx=mx: e.reduce_max(mx, bank[7][:, 0:T], AX), ts_, pb_free[s])
                    k = TS(mx, mx, -1.0, None, ALU.mult, None, k)
                    k = A(P, bank[7][:, 0:T], ACT.Exp, k, bias=mx, accum_out=sm)
                    bfree[7] = [k]
                    yield
                    k = dve.do(lambda e, n, sm=sm: e.reciprocal(sm, sm), k)
                    k = TS(P, P, sm, None, ALU.mult, None, k)

                    def tr(e, n, P=P):
                        for m in range(2):
                            ins = e.transpose(bank[7][:, 256 + m * 128:256 + m * 128 + 128], P[:, m * 128:m * 128 + 128], ident)
                        return ins

                    yield
                    k = pe.do(tr, k, t_id, bfree[7])
                    pb_free[s] = [k]
                    k = A(pT[:, :, s * 128:s * 128 + 128], bank[7][:, 256:512].rearrange("p (m t) -> p m t", m=2),
                          ACT.Copy, k, pt_free)
                    bfree[7] = [k]
                    pt.append(k)
                    yield
                last = []
                for d in range(2):
                    t = 2 * h + d

                    def pv(e, n, t=t):
                        for m in range(2):
                            ins = e.matmul(bank[7][:, 0:T], Vn[:, m, t * 128:t * 128 + 128], pT[:, m, :],
                                           start=m == 0, stop=m == 1)
                        return ins

                    k = pe.do(pv, pt, kv["V"], bfree[7])
                    last.append(k)
                    k = A(qT[:, t, :], bank[7][:, 0:T], ACT.Copy, k)
                    bfree[7] = [k]
                    o_tok[t] = k
                    yield
                pt_free = last
            state["att_done"] = [last, pb_free, k]
        background.insert(0, gen())

    def wait_attention():
        while o_tok[7] is None or "att_done" not in state:
            step()

    def ev_xg(t):
        def f(bk, done):
            r, ks = gated(bk, done, o_tok[t], qT[:, t, :], yx, t, state["att_done"])
            state["xg_done"] = ks
            return r
        return f

    gate = {}
    mg_tok = [None] * 16

    def ev_gate(t):
        def f(bk, done):
            si, s, fr = scr.next()
            k, rd = comb(bk, done, s, fr)
            gate[t] = (si, s, A(s, s, ACT.Tanh, k, scale=0.5))
            return rd
        return f

    def ev_branch(t, first):
        def f(bk, done):
            si, s, kg = gate[t]
            if first:
                k, rd = comb(bk, done, Mf[:, t, :], state["zb_done"])
                k = STT(Mf[:, t, :], s, 1.0, Mf[:, t, :], ALU.add, ALU.mult, k, kg)
                mg_tok[t] = k
                scr.free[si] = [k]
                return rd
            si2, s2, fr = scr.next()
            k, rd = comb(bk, done, s2, fr)
            k = STT(s2, s, 1.0, s2, ALU.add, ALU.mult, k, kg)
            k2 = TT(Mf[:, t, :], Mf[:, t, :], s2, ALU.add, k, mg_tok[t])
            scr.free[si] = [k]
            scr.free[si2] = [k2]
            mg_tok[t] = k2
            return rd
        return f

    mgp = Pair(Yr[:, 0:32, :], 16)

    def ev_branch_last(t):
        def f(bk, done):
            r = ev_branch(t, False)(bk, done)
            split(Mf[:, t:t + 1, :], mgp, t, 1, [mg_tok[t], state["yx_done"], state["glu_done"]], scale=0.5)
            return r
        return f

    def ev_glu(t):
        def f(bk, done):
            si, s, fr = scr.next()
            k0, rd = comb(bk, done, s, fr)
            k = TS(s, s, cv("glub", t), 0.5, ALU.add, ALU.mult, k0)
            k1 = A(s, s, ACT.Tanh, k)
            k2 = STT(uT[:, t, :], s, 1.0, uT[:, t, :], ALU.add, ALU.mult, k1, s5y[t])
            scr.free[si] = [k2]
            av["glu", t] = k2
            return rd
        return f

    def ev_bg(t):
        def f(bk, done):
            si, s, fr = scr.next()
            k0, rd = comb(bk, done, s, fr)
            k1 = A(s, s, ACT.Silu, k0)
            k3 = TT(s, s, uT[:, t, :], ALU.mult, k1, av["glu", t])
            ks = split(s.rearrange("p (o t) -> p o t", o=1), yb, t, 1, [k3, s5["work_done"]], scale=0.5)
            scr.free[si] = ks
            return rd
        return f

    W = a
    def call(fn):
        jobs.append(("call", 0, None, fn))

    def ensure(*keys):
        def f():
            while not all(k in state for k in keys):
                step()
        return f

    def mark_pe(name):
        def f():
            state[name] = [(pe.sem, pe.n)]
        return f

    for t in range(8):
        job("W", W["w_bx"], t, 2, hp, ev_bx(t))
    call(ensure("mem_done"))
    for t in range(8):
        job("W", W["w_k"], t, 2, mp, ev_k(t))
    for g in range(2):
        job("M", W["w_v"], g, 8, mp, ev_v(g))
    call(mark_pe("kv_done"))
    call(ensure("s5_ready"))
    for g in range(2):
        job("M", W["w_av"], g, 8, hp, ev_av(g))
    call(spatial)
    for t in range(8):
        job("W", W["w_q"], t, 2, hp, ev_q(t))
    call(ensure("sg_done"))
    for t in range(8):
        job("W", W["w_au"], t, 2, hp, ev_au(t))
        job("W", W["w_ag"], t, 2, hp, ev_ag(t))
    call(attention)
    for t in range(16):
        job("W", W["w_g0"], t, 2, hp, ev_gate(t))
        job("W", W["w_b0"], t, 1, ya, ev_branch(t, True))
    call(mark_pe("ya_done"))
    call(ensure("att_done"))
    for t in range(8):
        job("W", W["w_xg"], t, 2, hp, ev_xg(t))
    for t in range(16):
        job("W", W["w_g2"], t, 2, hp, ev_gate(t))
        job("W", W["w_b2"], t, 1, yx, ev_branch(t, False))
    call(drain)
    call(mark_pe("yx_done"))
    for t in range(8):
        job("W", W["w_glu"], t, 1, gp, ev_glu(t))

    def after_glu():
        state["glu_done"] = [(pe.sem, pe.n)]
    call(after_glu)
    for t in range(8):
        job("W", W["w_bg"], t, 2, hp, ev_bg(t))
    for t in range(16):
        job("W", W["w_g1"], t, 2, hp, ev_gate(t))
        job("W", W["w_b1"], t, 1, yb, ev_branch_last(t))

    acc = {}

    def square_sum(src, w, key, q=None):
        si, s, fr = scr2.next()
        k = A(s, src, ACT.Square, w, fr)
        dst = keep[key[1]]
        if acc.get(key) is None:
            k2 = TS(dst, s, 1.0, None, ALU.mult, None, k, acc.get(("free", key[1])))
        else:
            k2 = TT(dst, dst, s, ALU.add, k, acc[key])
        acc[key] = k2
        scr2.free[si] = [k2]
        return k

    f_tok = [None] * 16

    def ev_out(t):
        def f(bk, done):
            if t == 0:
                act.plain(lambda e, n: e.preload_act_table(ACT.Sqrt))
            si, s, fr = scr2.next()
            k, rd = comb(bk, done, s, fr, state["F_free"])
            k2 = square_sum(s, k, ("post", 0))
            f_tok[t] = A(F0[:, t, :], s, ACT.Copy, k, state["F_free"], scale=cv("post", t))
            scr2.free[si] = [f_tok[t], k2]
            return rd
        return f

    t_x2 = []

    def reload_x():
        state["F_free"] = [yb.tok, state["att_done"], s5["work_done"]]
        t_x2.append(load(sp, "xagain", [(Xf[:, :, :], a["xT"])], state["xg_done"]))
    call(reload_x)
    for t in range(16):
        job("W", W["w_out"], t, 2, mgp, ev_out(t))

    x_tok = [None] * 16
    h1 = Pair(Hr, 16)
    one = lambda ap: ap.rearrange("p (o t) -> p o t", o=1)

    def post():
        tr = rstd_of(keep[0], keep[1], 1e-6, acc["post", 0], None)
        sq, war = [], [(pe.sem, pe.n), mg_tok, mgp.tok]
        for t0, nt in ((0, 2), (2, 2), (4, 4), (8, 4), (12, 2), (14, 2)):
            f, x = F0[:, t0:t0 + nt, :], Xf[:, t0:t0 + nt, :]
            k = TT(f, f, one(keep[1]).broadcast_to((128, nt, T)), ALU.mult, tr, f_tok[t0:t0 + nt])
            k = TT(x, x, f, ALU.add, k, t_x2)
            for t in range(t0, t0 + nt):
                x_tok[t] = k
                sq.append(None)
            k = A(f, x, ACT.Square, k)
            for t in range(t0, t0 + nt):
                sq[t] = k

        def msum(e, n):
            for t in range(16):
                n(sq[t])
                ins = e.matmul(bank[7][:, 0:T], ones, F0[:, t, :], start=t == 0, stop=t == 15)
            return ins
        tm = pe.do(msum, bfree[7])
        tr = rstd_of(None, keep[3], 1e-5, None, None, tm=tm)
        act.plain(lambda e, n: e.preload_act_table(ACT.Tanh))
        for t in range(16):
            k = STT(Mf[:, t, :], Xf[:, t, :], cv("mix", t), keep[3], ALU.mult, ALU.mult, tr, x_tok[t], war)
            split(Mf[:, t:t + 1, :], h1, t, 1, [k, war])
        state["h1"] = [tm, h1.tok[15]]
    call(post)

    hb = small[:, 16:32]
    pads = Slots(upad)
    conv_in = {}
    c_tok = [None] * 16

    def ev_a(t):
        def f(bk, done):
            si, s, fr = scr2.next()
            conv_in[t] = (si, s, A(s, bk, ACT.Identity, done, fr, bias=cv("bpw1", t)))
            return [conv_in[t][2]]
        return f

    def ev_gt(t):
        def f(bk, done):
            if t == 0:
                state["hb"] = TS(hb, cvs("bpw1")[:, 16:32], 0.5, None, ALU.mult, None)
            si, s, fr = scr2.next()
            kt = A(s, bk, ACT.Tanh, done, fr, state["hb"], scale=0.5, bias=hb[:, t:t + 1])
            sa, sap, ka = conv_in[t]
            while t >= 4 and c_tok[t - 4] is None:
                step()
            pi, pad, pf = pads.next()
            if t < 4:
                z1 = dve.do(lambda e, n: e.memset(pad, 0.0), state["h1"], x_tok[15])
            else:
                z1 = None
            ku = STT(pad[:, 15:271], s, 1.0, sap, ALU.add, ALU.mult, kt, ka, pf, z1)
            scr2.free[si] = [ku]
            scr2.free[sa] = [ku]
            conv_in["u", t] = (pi, pad, ku)
            if t % 2:
                background.append(conv(t - 1))
            return [kt]
        return f

    def conv(t0):
        while t0 and c_tok[t0 - 1] is None:
            yield
        ks = [None, None]
        ac = [bank[4 + i][:, 0:T] for i in range(2)]
        for j in range(31):
            for i in range(2):
                t = t0 + i
                pi, pad, ku = conv_in["u", t]
                wj = cst[:, C_OFF["wdw"][0] + t * 31 + j:C_OFF["wdw"][0] + t * 31 + j + 1]
                if j == 0:
                    ks[i] = TS(ac[i], pad[:, j:j + T], wj, cv("bdw", t), ALU.mult, ALU.add, ku, state["h1"], state["wdw"],
                               bfree[4 + i])
                else:
                    dst = ac[i] if j < 30 else Mf[:, t, :]
                    ks[i] = STT(dst, pad[:, j:j + T], wj, ac[i], ALU.mult, ALU.add, ks[i])
            if j % 4 == 3:
                yield
        for i in range(2):
            pads.free[conv_in["u", t0 + i][0]] = [ks[i]]
            c_tok[t0 + i] = ks[i]
            bfree[4 + i] = [ks[i]]

    def halve_w():
        state["F1_free"] = [(pe.sem, pe.n), (dve.sem, dve.n), (act.sem, act.n)]
        state["wdw"] = TS(cvs("wdw"), cvs("wdw"), 0.5, None, ALU.mult, None, t_c)
    call(halve_w)
    c_p1 = len(chunks)
    for t in range(16):
        job("T", W["w_p1"], t, 2, h1, ev_a(t))
        job("T", W["w_p1"], 16 + t, 2, h1, ev_gt(t))
    pool_chunks.update(range(c_p1, len(chunks)))
    cp = Pair(Yr[:, 0:32, :], 16)

    def until(i):
        while c_tok[i] is None:
            step()

    def ln2():
        act.plain(lambda e, n: e.preload_act_table(ACT.Sqrt))
        mA, m1, m2, rs = keep
        until(13)

        def msum(bk, src, t0, t1, waits, scale_last):
            def f(e, n):
                for t in range(t0, t1):
                    for x in flat(waits[t]):
                        n(x)
                    ins = e.matmul(bank[bk][:, 0:T], ones, src[:, t, :], start=t == 0, stop=t == scale_last)
                return ins
            return pe.do(f, t_ones, bfree[bk] if t0 == 0 else None)

        km = msum(7, Mf, 0, 14, c_tok, 13)
        km = A(mA, bank[7][:, 0:T], ACT.Copy, km, scale=2048.0 / (14 * 128))
        bfree[7] = [km]
        kc, ks = [None] * 16, [None] * 16

        def centre(t0, nt):
            m = Mf[:, t0:t0 + nt, :]
            k = TT(m, m, one(mA).broadcast_to((128, nt, T)), ALU.subtract, km, c_tok[t0:t0 + nt])
            k2 = A(F1[:, t0:t0 + nt, :], m, ACT.Square, k, state["F1_free"])
            for t in range(t0, t0 + nt):
                kc[t], ks[t] = k, k2

        for t0, nt in ((0, 4), (4, 4), (8, 4), (12, 2)):
            centre(t0, nt)
            step()
        until(15)
        msum(7, Mf, 0, 14, kc, 15)
        msum(6, F1, 0, 14, ks, 15)
        centre(14, 2)
        k1 = msum(7, Mf, 14, 16, kc, 15)
        k2 = msum(6, F1, 14, 16, ks, 15)
        k1 = A(m1, bank[7][:, 0:T], ACT.Copy, k1)
        bfree[7] = [k1]
        k = TT(m2, m1, m1, ALU.mult, k1)
        k = STT(m2, bank[6][:, 0:T], 1e-5, m2, ALU.add, ALU.subtract, k2, k)
        bfree[6] = [k]
        k = A(m2, m2, ACT.Sqrt, k)
        k = dve.do(lambda e, n: e.reciprocal(rs, m2), k)
        act.plain(lambda e, n: e.preload_act_table(ACT.Silu))
        for t0 in range(0, 16, 2):
            m = Mf[:, t0:t0 + 2, :]
            ka = TT(m, m, one(m1).broadcast_to((128, 2, T)), ALU.subtract, k1, kc[t0:t0 + 2])
            ka = TT(m, m, one(rs).broadcast_to((128, 2, T)), ALU.mult, ka, k)
            kk = [A(Mf[:, t, :], Mf[:, t, :], ACT.Silu, ka, scale=cv("lng", t), bias=cv("lnb", t))
                  for t in (t0, t0 + 1)]
            split(m, cp, t0, 2, kk)
        state["cp"] = cp.tok[15]
    call(ln2)

    h2 = Pair(Hr, 16)

    def ev_p2(t):
        def f(bk, done):
            k = STT(Xf[:, t, :], bk[:, 0:T], cv("bpw2", t), Xf[:, t, :], ALU.add, ALU.add, done, x_tok[t])
            k = TT(Xf[:, t, :], Xf[:, t, :], bk[:, T:2 * T], ALU.add, k)
            x_tok[t] = k
            ka = A(h2.hi[:, t, :], Xf[:, t, :], ACT.Copy, k, scale=cv("ffn", t))
            kd = STT(h2.lo[:, t, :], Xf[:, t, :], cv("ffn", t), h2.hi[:, t, :].bitcast(F32), ALU.mult, ALU.subtract, ka)
            h2.tok[t] = [ka, kd]
            square_sum(Xf[:, t, :], k, ("ffn", 0))
            if t == 0:
                act.plain(lambda e, n: e.preload_act_table(ACT.Sqrt))
            return [k]
        return f

    for t in range(16):
        job("W", W["w_p2"], t, 2, cp, ev_p2(t))

    def pre_ffn():
        state["r_ffn"] = rstd_of(keep[0], keep[1], 1e-5, acc["ffn", 0], None)
    call(pre_ffn)

    hid = [Pair(Yr[:, 0:32, :], 16) for _ in range(4)]

    def ev_up(q, t):
        def f(bk, done):
            si, s, fr = scr2.next()
            k, rd = comb(bk, done, s, fr)
            k = TT(s, s, keep[1], ALU.mult, k, state["r_ffn"])
            k2 = STT(s, s, 0.0, s, ALU.max, ALU.mult, k)
            ks = split(s.rearrange("p (o t) -> p o t", o=1), hid[q], t, 1, [k2, state["war_hid"]])
            scr2.free[si] = ks
            return rd
        return f

    def ev_dn(q, t):
        def f(bk, done):
            k = TT(Xf[:, t, :], Xf[:, t, :], bk[:, 0:T], ALU.add, done, x_tok[t])
            k = TT(Xf[:, t, :], Xf[:, t, :], bk[:, T:2 * T], ALU.add, k)
            x_tok[t] = k
            if q == 3:
                square_sum(Xf[:, t, :], k, ("fin", 2))
            return [k]
        return f

    def mark():
        state["war_hid"] = [(pe.sem, pe.n)]

    for q in range(4):
        call(mark)
        for t in range(16):
            job("W", W["w_up"], 16 * q + t, 2, h2, ev_up(q, t))
        for t in range(16):
            job("W", W["w_dn"], 16 * q + t, 2, hid[q], ev_dn(q, t))

    s_out = sem("s_out")

    def finish():
        tr = rstd_of(keep[2], keep[3], 1e-5, acc["fin", 2], None)
        for i in range(4):
            for t in range(4 * i, 4 * i + 4):
                k = STT(Xf[:, t, :], Xf[:, t, :], cv("fin", t), keep[3], ALU.mult, ALU.mult, tr, x_tok[t])
            tok = sp.dma(lambda e, n, i=i: e.dma_start(out[:, 4 * i:4 * i + 4, :], Xf[:, 4 * i:4 * i + 4, :]),
                         s_out, 16 * (i + 1), k)
        sp.only_wait(tok)
    call(finish)

    state["declared"] = True
    for _ in norm_in(Xf, t_x, "pre", hp, sq0, 1e-6, None, fast=True):
        pass
    state["x_done"] = state["normed"]

    def early():
        yield
        yield from norm_in(Mf, [t_mem] * 4, "memg", mp, sq0, 1e-6, state["x_done"])
        state["mem_done"] = state["normed"]
        yield from s5_setup()
        yield from s5_main()
        yield from s5_gelu()

    background.append(early())
    run_jobs()
    drain()

    with nc.Block() as block:
        @block.sync
        def _(e):
            sp.emit(e)

        @block.gpsimd
        def _(e):
            pool.emit(e)

        @block.scalar
        def _(e):
            act.emit(e)

        @block.vector
        def _(e):
            dve.emit(e)

        @block.tensor
        def _(e):
            pe.emit(e)


def kernel(**x):
    import concourse.bacc as bacc
    from concourse.bass_utils import run_bass_kernel_spmd

    f = np.float32

    def cols(v):
        return np.asarray(v).reshape(-1, 128).T

    def tilesT(w):
        k, n = w.shape
        return np.ascontiguousarray(w.reshape(k // 1024, 8, 128, n // 128, 128).transpose(3, 0, 2, 1, 4)
                                    .reshape(n // 128, k // 1024, 128, 1024))

    def tilesM(w):
        k, n = w.shape
        return np.ascontiguousarray(w.reshape(k // 256, 2, 128, n // 512, 512).transpose(3, 0, 2, 1, 4)
                                    .reshape(n // 512, k // 256, 128, 1024))

    def actT(v):
        return np.ascontiguousarray(v[0].reshape(256, 16, 128).transpose(2, 1, 0))

    x = {k: np.asarray(v) for k, v in x.items()}
    pg = lambda v: v.reshape(32, 2, 64).transpose(1, 2, 0).reshape(128, 32)
    ldt = np.ascontiguousarray(np.broadcast_to(x["ssm_log_dt"][0][:, None], (64, 64)))
    wdw = x["conv_w_dw_2"][0].reshape(31, 16, 128).transpose(2, 1, 0).reshape(128, 496)
    parts = {
        "pre": cols(x["pre_norm_g"][0]), "memg": cols(x["mem_norm_g"][0]), "post": cols(x["post_norm_g"][0]),
        "glub": cols(x["glu_b"][0]), "d": cols(x["ssm_d"][0]), "mix": cols(x["norm_mix_g_2"][0]),
        "ffn": cols(x["norm_ffn_g_2"][0]), "fin": cols(x["final_norm_g_2"]), "bpw1": cols(x["conv_b_pw1_2"][0]),
        "bdw": cols(x["conv_b_dw_2"][0]), "lng": cols(x["conv_ln_g_2"][0]), "lnb": cols(x["conv_ln_b_2"][0]),
        "bpw2": cols(x["conv_b_pw2_2"][0]), "wdw": wdw, "are": pg(x["ssm_a_re"][0]), "aim": pg(x["ssm_a_im"][0]),
        "ldt": pg(ldt), "iota": np.ascontiguousarray(np.broadcast_to(np.arange(16, dtype=f), (128, 16))),
    }
    cst = np.ascontiguousarray(np.concatenate([parts[k] for k in C_OFF], axis=1))
    BT = np.zeros((128, 2, 8, 128), f)
    CT = np.zeros((128, 2, 32, 32), f)
    for r, (bn, cn) in enumerate((("ssm_b_re", "ssm_c_re"), ("ssm_b_im", "ssm_c_im"))):
        b = x[bn][0].reshape(8, 4, 2, 64, 16)
        c = x[cn][0].reshape(32, 2, 16, 64)
        for g in range(2):
            for q in range(4):
                BT[32 * q + 16 * g:32 * q + 16 * g + 16, r, :, 64 * g:64 * g + 64] = b[:, q, g].transpose(2, 0, 1)
            CT[64 * g:64 * g + 64, r, :, 16 * g:16 * g + 16] = c[:, g].transpose(2, 0, 1)
    w_in = x["w_in"][0]
    seg = lambda i: w_in[:, 1024 * i:1024 * (i + 1)]
    gts = lambda i: w_in[:, 7168 + 2048 * i:7168 + 2048 * (i + 1)]
    wd = x["ffn_w_down_2"][0]
    arrays = {
        "xT": actT(x["x"]), "memT": actT(x["mem"]), "cst": cst, "BT": BT, "CT": CT,
        "sgw": np.ascontiguousarray(x["sg_w"][0].transpose(2, 0, 1)),
        "sgb": np.ascontiguousarray(np.broadcast_to(x["sg_b"][0], (128, 8, 128))),
        "lng": np.ascontiguousarray(np.broadcast_to(x["sg_ln_g"][0], (128, 1024))),
        "lnb": np.ascontiguousarray(np.broadcast_to(x["sg_ln_b"][0], (128, 1024))),
        "w_au": tilesT(seg(0)), "w_av": tilesM(seg(1)), "w_ag": tilesT(seg(2)), "w_bx": tilesT(seg(3)),
        "w_bg": tilesT(seg(4)), "w_q": tilesT(seg(5)), "w_xg": tilesT(seg(6)),
        "w_g0": tilesT(gts(0)), "w_g1": tilesT(gts(1)), "w_g2": tilesT(gts(2)),
        "w_k": tilesT(x["xa_wk"][0]), "w_v": tilesM(x["xa_wv"][0]), "w_glu": tilesT(x["glu_w"][0]),
        "w_b0": tilesT(x["w_branch"][0, 0]), "w_b1": tilesT(x["w_branch"][0, 1]), "w_b2": tilesT(x["w_branch"][0, 2]),
        "w_out": tilesT(x["w_out"][0]), "w_p1": tilesT(x["conv_w_pw1_2"][0]), "w_p2": tilesT(x["conv_w_pw2_2"][0]),
        "w_up": tilesT(x["ffn_w_up_2"][0]),
        "w_dn": np.concatenate([tilesT(wd[2048 * i:2048 * (i + 1)]) for i in range(4)]),
    }
    nc = bacc.Bacc("TRN2", target_bir_lowering=False, num_devices=1)
    aps = {k: nc.dram_tensor(f"in_{k}", v.shape, mybir.dt.from_np(v.dtype), kind="ExternalInput").ap()
           for k, v in arrays.items()}
    out = nc.dram_tensor("out_y", (128, 16, 256), F32, kind="ExternalOutput").ap()
    hybrid(nc, aps, out)
    r = run_bass_kernel_spmd(nc, [{f"in_{k}": v for k, v in arrays.items()}], core_ids=[0])
    y = r.results[0]["out_y"]
    return np.ascontiguousarray(y.transpose(2, 1, 0).reshape(1, 256, 2048))
```

```python
import math
from contextlib import ExitStack

import numpy as np

import concourse.bass as bass
from concourse import mybir

F32 = mybir.dt.float32
F32R = mybir.dt.float32r
I32 = mybir.dt.int32
ALU = mybir.AluOpType
ACT = mybir.ActivationFunctionType
AX = mybir.AxisListType.X

T = 256
KB = 256
RAW, WN = 7, 4
CH = 1024
MAGIC = 12582912.0

C_OFF = {}
_n = 0
for _name, _w in (("pre", 16), ("memg", 16), ("post", 16), ("glub", 8), ("d", 8), ("mix", 16), ("ffn", 16),
                  ("fin", 16), ("bpw1", 32), ("bdw", 16), ("lng", 16), ("lnb", 16), ("bpw2", 16),
                  ("glng", 8), ("glnb", 8), ("wdw", 496), ("are", 32), ("aim", 32), ("ldt", 32), ("iota", 16)):
    C_OFF[_name] = (_n, _w)
    _n += _w
NCONST = _n


class Queue:

    def __init__(self, name, sem):
        self.name, self.sem, self.n, self.ops = name, sem, 0, []

    def do(self, fn, *waits):
        self.n += 1
        self.ops.append((waits, fn, (self.sem, 1)))
        return (self.sem, self.n)

    def dma(self, fn, sem, value, *waits):
        self.ops.append((waits, fn, (sem, 16)))
        return (sem, value)

    def plain(self, fn):
        self.ops.append(((), fn, None))

    def only_wait(self, *waits):
        self.ops.append((waits, None, None))

    def emit(self, eng):
        seen = {}

        def need(tok):
            sem, v = tok
            if seen.get(id(sem), 0) < v:
                eng.wait_ge(sem, v)
                seen[id(sem)] = v

        for waits, fn, inc in self.ops:
            for w in flat(waits):
                need(w)
            if fn is not None:
                ins = fn(eng, need)
                if inc is not None:
                    ins.then_inc(*inc)


def flat(x):
    if x is None:
        return
    if isinstance(x, list) or (isinstance(x, tuple) and (not x or isinstance(x[0], (tuple, list)) or x[0] is None)):
        for y in x:
            yield from flat(y)
    else:
        yield x


class Slots:

    def __init__(self, aps):
        self.aps, self.free, self.i = aps, [[] for _ in aps], -1

    def next(self):
        for _ in self.aps:
            self.i = (self.i + 1) % len(self.aps)
            if self.free[self.i] is not None:
                break
        free = self.free[self.i]
        assert free is not None
        self.free[self.i] = None
        return self.i, self.aps[self.i], free


class Pair:

    def __init__(self, both, n):
        self.hi, self.lo, self.tok = both[:, 0:n, :], both[:, n:2 * n, :], [None] * n
        self.both = both.rearrange("p (h n) t -> p h n t", h=2)


def hybrid(nc, a, out):
    with ExitStack() as ctx:
        _build(nc, a, out, ctx)


def _build(nc, a, out, ctx):
    def sem(name):
        return ctx.enter_context(nc.semaphore(name))

    ctx.enter_context(nc.sbuf_tensor("arena", [128, 212800 // 4], F32))
    base = 16512

    def at(name, off, n, dt=F32):
        return nc.alloc_sbuf_tensor_at(name, [128, n], dt, offset=base + off)[:, :]

    K1 = 1024
    o_raw, o_wh = 0, RAW * 4 * K1
    o_H = (RAW + WN) * 4 * K1
    o_YA = o_H + 32 * K1
    o_YX = o_YA + 16 * K1
    o_YB = o_YX + 16 * K1
    o_X = o_YB + 16 * K1
    o_M = o_X + 16 * K1
    o_F = o_M + 16 * K1
    o_C = o_F + 40 * K1
    raw = at("raw", o_raw, RAW * CH).rearrange("p (s n) -> p s n", s=RAW)
    wh = at("wh", o_wh, WN * CH, F32R).rearrange("p (s n) -> p s n", s=WN)
    wl = at("wl", o_raw, RAW * CH, F32R).rearrange("p (s n) -> p s n", s=RAW)

    def tiles(name, off, n, dt=F32):
        return at(name, off, n * T, dt).rearrange("p (n t) -> p n t", t=T)

    Hr = tiles("Hr", o_H, 32, F32R)
    Yr = tiles("Yr", o_YA, 48, F32R)
    Xf = tiles("Xf", o_X, 16)
    Mf = tiles("Mf", o_M, 16)
    cst = at("cst", o_C, NCONST)
    o = o_C + NCONST * 4
    ones = at("ones", o, 128)
    ident = at("ident", o + 512, 128)
    small = at("small", o + 1024, 64)
    o += 1024 + 256
    nscr = 4
    assert o + (nscr + 2) * 1024 <= 212800, o
    scr = Slots([at(f"scr{i}", o + i * 1024, T) for i in range(nscr)])
    Vn = at("Vn", o_F, 2048).rearrange("p (m n) -> p m n", m=2)
    uT = tiles("uT", o_F + 8 * K1, 8)
    Bs = at("Bs", o_F + 16 * K1, 2048).rearrange("p (r t n) -> p r t n", r=2, t=8)
    Cs = at("Cs", o_F + 24 * K1, 2048).rearrange("p (r k n) -> p r k n", r=2, k=32)
    tab = at("tab", o_F + 32 * K1, 2048).rearrange("p (s w k n) -> p s w k n", s=2, w=2, k=32)
    sq0 = tiles("sq0", o_YB, 16)
    ang = at("ang", o_YB, 1024)
    angt = at("angt", o_YB + 4 * K1, 1024)
    ct = at("ct", o_YB + 8 * K1, 2048).rearrange("p (r k n) -> p r k n", r=2, k=32)
    sv = at("sv", o_X + 8 * K1, 40 * 32).rearrange("p (i n) -> p i n", n=32)
    wcs = [at(f"wcs{i}", o_YB + 2 * i * K1, 512).rearrange("p (r t) -> p r t", r=2) for i in range(2)]
    wsc = at("wsc", o_YB + 4 * K1, 512).rearrange("p (r t) -> p r t", r=2)
    wpt = at("wpt", o_YB + 6 * K1, 512).rearrange("p (r t) -> p r t", r=2)
    wm1 = at("wm1", o_YB + 8 * K1, 512).rearrange("p (r t) -> p r t", r=2)
    wm2 = at("wm2", o_YB + 10 * K1, 512).rearrange("p (r t) -> p r t", r=2)
    wn1 = at("wn1", o_YB + 12 * K1, 512).rearrange("p (r t) -> p r t", r=2)
    wn2 = at("wn2", o_YB + 14 * K1, 512).rearrange("p (r t) -> p r t", r=2)
    sgw = at("sgw", o_F, 1024).rearrange("p (g t) -> p g t", g=8)
    sgb = at("sgb", o_F + 4 * K1, 1024).rearrange("p (g t) -> p g t", g=8)
    qT = tiles("qT", o_X, 8)
    KT = tiles("KT", o_X + 8 * K1, 8)
    vn = at("vn", o_M, 2048).rearrange("p (c n) -> p c n", c=2)
    zb = tiles("zb", o_M + 8 * K1, 8)
    Pb = [at(f"Pb{i}", o + (nscr + i) * 1024, T) for i in range(2)]
    pT = at("pT", o_YX, 512).rearrange("p (m t) -> p m t", m=2)
    F0 = tiles("F0", o_F, 16)
    upad = [at(f"upad{i}", o_F + 28 * K1 + i * 1152, 286) for i in range(4)]
    F1 = tiles("F1", o_H, 16)
    extra = [at(f"extra{i}", o_F + (33 + i) * K1, T) for i in range(2)]
    dg = [[at(f"dg{i}{h}", o, 31 * 128, F32R).rearrange("p (j n) -> p j n", j=31) for h, o in enumerate(oo)]
          for i, oo in enumerate(((o_YA, o_YA + 31 * 512), (o_YA + 62 * 512, o_F)))]
    ub = [[at(f"ub{i}{h}", o_F + 33 * K1 + (2 * i + h) * 1152, 286, F32R) for h in range(2)] for i in range(2)]
    w62 = [at(f"w62{i}", o_F + 38 * K1 + i * 256, 62, d) for i, d in enumerate((F32R, F32))]
    keep = [at(f"keep{i}", o_F + 16 * K1 + i * K1, T) for i in range(4)]
    scr2 = Slots([at(f"scrB{i}", o_F + 20 * K1 + i * K1, T) for i in range(8)])

    bank = [ctx.enter_context(nc.psum_tensor(f"bank{i}", [128, 512], F32))[:, :] for i in range(8)]
    bfree = [[] for _ in range(8)]

    pe = Queue("pe", sem("s_pe"))
    act = Queue("act", sem("s_act"))
    dve = Queue("dve", sem("s_dve"))
    pool = Queue("pool", sem("s_pool"))
    sp = Queue("sp", sem("s_sp"))
    s_raw = [sem(f"s_raw{i}") for i in range(RAW)]

    def load(q, name, pairs, *waits):
        s = sem("s_" + name)
        for dst, src in pairs:
            tok = q.dma(lambda e, n, dst=dst, src=src: e.dma_start(dst, src), s, 16 * len(pairs), *waits)
        return tok

    def cv(name, i=0):
        off = C_OFF[name][0] + i
        return cst[:, off:off + 1]

    def cvs(name):
        off, w = C_OFF[name]
        return cst[:, off:off + w]

    def A(dst, src, func, *w, **kw):
        return act.do(lambda e, n: e.activation(dst, src, func, **kw), *w)

    def TT(dst, x, y, op, *w, q=None):
        return (q or dve).do(lambda e, n: e.tensor_tensor(dst, x, y, op), *w)

    def TS(dst, x, s1, s2, op0, op1, *w):
        if s2 is None:
            return dve.do(lambda e, n: e.tensor_scalar(dst, x, s1, None, op0), *w)
        return dve.do(lambda e, n: e.tensor_scalar(dst, x, s1, s2, op0, op1), *w)

    def STT(dst, x, s, y, op0, op1, *w):
        return dve.do(lambda e, n: e.scalar_tensor_tensor(dst, x, s, y, op0, op1), *w)

    def split(src, pair, t0, nt, waits, scale=None):
        hi, lo = pair.hi[:, t0:t0 + nt, :], pair.lo[:, t0:t0 + nt, :]
        kw = {} if scale is None else {"scale": scale}
        ta = A(hi, src, ACT.Copy, waits, **kw)
        if scale is None:
            td = TT(lo, src, hi.bitcast(F32), ALU.subtract, ta)
        else:
            td = STT(lo, src, scale, hi.bitcast(F32), ALU.mult, ALU.subtract, ta)
        for t in range(t0, t0 + nt):
            pair.tok[t] = [ta, td]
        return [ta, td]

    def split_later(src, pair, t0, nt, waits):
        hi, lo = pair.hi[:, t0:t0 + nt, :], pair.lo[:, t0:t0 + nt, :]
        ta = A(hi, src, ACT.Copy, waits)

        def rest():
            td = TT(lo, src, hi.bitcast(F32), ALU.subtract, ta)
            for t in range(t0, t0 + nt):
                pair.tok[t] = [ta, td]
        return rest

    def comb(bk, done, dst, *w, scale=None):
        kw = {} if scale is None else {"scale": scale}
        ka = A(dst, bk[:, T:2 * T], ACT.Copy, done, *w, **kw)
        if scale is None:
            kd = TT(dst, dst, bk[:, 0:T], ALU.add, ka)
        else:
            kd = STT(dst, bk[:, 0:T], scale, dst, ALU.mult, ALU.add, ka)
        return kd, [ka, kd]

    chunks = []
    jobs = []

    def job(kind, w, idx, nch, acts, then):
        group((kind, w, idx, nch, acts, then))

    def group(*members, hooks={}):
        jobs.append(([(kind, nch, acts, then) for kind, w, idx, nch, acts, then in members], hooks))
        for c in range(members[0][3]):
            for kind, w, idx, nch, acts, then in members:
                chunks.append(w[idx, c, :, :])

    split_tok = {}
    pool_chunks = set()
    pe_tok = {}
    dma_tok = {}
    state = {"late": False, "split": 0, "dma": 0, "declared": False}

    def dma_chunk():
        c = state["dma"]
        if state["declared"] and c >= len(chunks):
            return
        s = c % RAW
        waits = [] if c < RAW else [pe_tok[c - RAW]]
        dma_tok[c] = sp.dma(lambda e, n, c=c, s=s: e.dma_start(raw[:, s, :], chunks[c]),
                            s_raw[s], 16 * (c // RAW + 1), waits)
        state["dma"] += 1

    def split_chunk():
        c = state["split"]
        if c >= len(chunks):
            return
        r, s = c % RAW, c % WN
        free = pe_tok[c - WN] if c >= WN else None
        ta = A(wh[:, s, :], raw[:, r, :], ACT.Copy, dma_tok[c], free)
        on = pool if c in pool_chunks else dve
        td = TT(wl[:, r, :], raw[:, r, :], wh[:, s, :].bitcast(F32), ALU.subtract, dma_tok[c], ta, q=on)
        split_tok[c] = [ta, td]
        state["split"] += 1

    def mm_tile(e, need, s, r, k0, pr, dst, first, last, wide):
        for kk in range(8):
            k = k0 + kk
            for t in flat(pr.tok[k]):
                need(t)
            lh = wh[:, s, kk * 128:kk * 128 + 128]
            ll = wl[:, r, kk * 128:kk * 128 + 128]
            if wide:
                e.matmul(dst.rearrange("p (h t) -> p h t", h=2), lh, pr.both[:, :, k, :], start=first and kk == 0,
                         stop=last and kk == 7, skip_group_check=True)
                ins = e.matmul(dst[:, 0:T], ll, pr.hi[:, k, :], start=False, stop=last and kk == 7,
                               skip_group_check=True)
            else:
                e.matmul(dst[:, 0:T], lh, pr.hi[:, k, :], start=first and kk == 0, stop=False)
                e.matmul(dst[:, 0:T], lh, pr.lo[:, k, :], start=False, stop=False)
                ins = e.matmul(dst[:, 0:T], ll, pr.hi[:, k, :], start=False, stop=last and kk == 7)
        return ins

    def mm_rows(e, need, s, r, k0, pr, dsts, first, last):
        for kk in range(2):
            k = k0 + kk
            for t in flat(pr.tok[k]):
                need(t)
            rh = wh[:, s, kk * 512:kk * 512 + 512]
            rl = wl[:, r, kk * 512:kk * 512 + 512]
            for h in range(2):
                xh = pr.hi[:, k, h * 128:h * 128 + 128]
                xl = pr.lo[:, k, h * 128:h * 128 + 128]
                e.matmul(dsts[h], xh, rh, start=first and kk == 0, stop=False)
                e.matmul(dsts[h], xh, rl, start=False, stop=False)
                ins = e.matmul(dsts[h], xl, rh, start=False, stop=last and kk == 1)
        return ins

    background = []

    def step():
        for g in list(background):
            try:
                next(g)
            except StopIteration:
                background.remove(g)

    def drain():
        while background:
            step()

    def run_jobs():
        c = 0
        b = 0
        for entry in jobs:
            if callable(entry):
                entry()
                continue
            members, hooks = entry
            bs = []
            for m in members:
                n = 2 if m[0] == "M" else 1
                bs.append([(b + x) % 4 for x in range(n)])
                b += n
            units = [(i, m) for i in range(members[0][1]) for m in range(len(members))]
            for u, (i, m) in enumerate(units):
                kind, nch, acts, then = members[m]
                while state["split"] < min(c + WN, len(chunks)):
                    split_chunk()
                s = c % WN
                first, last = i == 0, i == nch - 1
                waits = [split_tok[c]] + ([bfree[x] for x in bs[m]] if first else [])
                if kind != "M":
                    dst = bank[bs[m][0]]
                    pe_tok[c] = pe.do(lambda e, n, s=s, r=c % RAW, k0=8 * i, acts=acts, dst=dst, f=first, l=last, w=kind == "W":
                                      mm_tile(e, n, s, r, k0, acts, dst, f, l, w), *waits)
                else:
                    dsts = [bank[x] for x in bs[m]]
                    pe_tok[c] = pe.do(lambda e, n, s=s, r=c % RAW, k0=2 * i, acts=acts, dsts=dsts, f=first, l=last:
                                      mm_rows(e, n, s, r, k0, acts, dsts, f, l), *waits)
                dma_chunk()
                c += 1
                if last:
                    if c < len(chunks) and state["split"] <= c + WN - 1 and not state["late"]:
                        split_chunk()
                    done = pe_tok[c - 1]
                    if kind == "T":
                        bfree[bs[m][0]] = then(bank[bs[m][0]][:, 0:T], done)
                    elif kind == "W":
                        bfree[bs[m][0]] = then(bank[bs[m][0]], done)
                    else:
                        for x, f in zip(bs[m], then([bank[x] for x in bs[m]], done)):
                            bfree[x] = f
                step()
                if u in hooks:
                    hooks[u]()

    x_load = lambda q, i: load(q, f"x{i}", [(Xf[:, 4 * i:4 * i + 4, :], a["xT"][:, 4 * i:4 * i + 4, :])])
    act.plain(lambda e, n: e.preload_act_table(ACT.Sqrt))
    t_c0 = load(sp, "cst0", [(cst[:, 0:16], a["cst"][:, 0:16])])
    t_x = [x_load(sp, 0), x_load(sp, 1)]
    dma_chunk()
    dma_chunk()
    t_x.append(x_load(sp, 2))
    dma_chunk()
    t_x.append(x_load(sp, 3))
    t_c = load(sp, "cst", [(cst[:, 16:NCONST], a["cst"][:, 16:NCONST])])
    while state["dma"] < RAW:
        dma_chunk()

    t_ones = dve.do(lambda e, n: e.memset(ones, 1.0 / 2048))
    t_i0 = pool.do(lambda e, n: e.memset(ident, 0.0))
    t_id = pool.do(lambda e, n: e.affine_select(out=ident, in_=ident, compare_op=ALU.not_equal, fill=1.0, base=0,
                                                pattern=[[-1, 128]], channel_multiplier=1), t_i0)

    def tree(buf, n, w):
        tok = w
        while n > 1:
            n //= 2
            tok = TT(buf[:, 0:n, :], buf[:, 0:n, :], buf[:, n:2 * n, :], ALU.add, tok)
        return tok

    def mean_of(src, w, bk=7):
        return pe.do(lambda e, n: e.matmul(bank[bk][:, 0:T], ones, src, start=True, stop=True), w, t_ones, bfree[bk])

    def rstd_of(src, dst, eps, w, wd, bk=7, tm=None):
        tm = tm or mean_of(src, w, bk)
        te = TS(dst, bank[bk][:, 0:T], eps, None, ALU.add, None, tm, wd)
        bfree[bk] = [te]
        ts_ = A(dst, dst, ACT.Sqrt, te)
        return dve.do(lambda e, n: e.reciprocal(dst, dst), ts_)

    hp = Pair(Hr, 16)
    mp = Pair(Yr[:, 0:32, :], 16)

    hp0 = Pair(Yr[:, 0:32, :], 16)
    r_x, r_mem = Pb[1], Pb[0]

    def start_x():
        sq = []
        for i in range(4):
            for t in range(4 * i, 4 * i + 4):
                ka = A(hp0.hi[:, t, :], Xf[:, t, :], ACT.Copy, t_x[i], t_c0, scale=cv("pre", t))
                kd = STT(hp0.lo[:, t, :], Xf[:, t, :], cv("pre", t), hp0.hi[:, t, :].bitcast(F32), ALU.mult,
                         ALU.subtract, ka)
                hp0.tok[t] = [ka, kd]
            if i < 3:
                split_chunk()
        for i in range(4):
            sq.append(A(sq0[:, 4 * i:4 * i + 4, :], Xf[:, 4 * i:4 * i + 4, :], ACT.Square, t_x[i]))
            if i == 1:
                split_chunk()
        state["x_sum"] = tree(sq0, 16, sq)

    def scaled(buf, gname, rs, tr, pair, free=None):
        tk, rest = {}, {}
        for t0 in range(0, 20, 2):
            if t0 < 16:
                tk[t0] = [STT(buf[:, t, :], buf[:, t, :], cv(gname, t), rs, ALU.mult, ALU.mult, tr, t_c)
                          for t in range(t0, t0 + 2)]
            if 2 <= t0 < 18:
                u = t0 - 2
                rest[u] = split_later(buf[:, u:u + 2, :], pair, u, 2, [tk[u], free])
            if t0 >= 4:
                rest[t0 - 4]()
            yield

    t_mem = [None] * 4

    def more_loads():
        for i in range(4):
            yield
            t_mem[i] = load(sp, f"mem{i}", [(Mf[:, 4 * i:4 * i + 4, :], a["memT"][:, 4 * i:4 * i + 4, :])])
            yield
        bc = []
        for r in range(2):
            bc.append(load(sp, f"b{r}", [(Bs[:, r, :, :], a["BT"][:, r, :, :])]))
            yield
            yield
            bc.append(load(sp, f"c{r}", [(Cs[:, r, :, :], a["CT"][:, r, :, :])]))
            yield
            yield
        state["bc"] = bc
        g1 = load(sp, "sgw", [(sgw[:, :, :], a["sgw"])])
        yield
        yield
        state["sg"] = [g1, load(sp, "sgb", [(sgb[:, :, :], a["sgb"])])]

    def early():
        for _ in range(8):
            if "want_rx" not in state:
                yield
        tr = rstd_of(sq0[:, 0, :], r_x, 1e-6, state["x_sum"], None)
        state["rx"] = tr
        yield from scaled(Xf, "pre", r_x, tr, hp)
        state["x_done"] = [hp.tok[15], hp0.tok]
        sq = []
        for i in range(4):
            while t_mem[i] is None:
                yield
            sq.append(A(sq0[:, 4 * i:4 * i + 4, :], Mf[:, 4 * i:4 * i + 4, :], ACT.Square, t_mem[i], tr))
            yield
        k = tree(sq0, 16, sq)
        yield
        yield
        yield
        tr = rstd_of(sq0[:, 0, :], r_mem, 1e-6, k, None)
        state["sq_done"] = tr
        background.append(s5_all())
        while "bx_done" not in state:
            yield
        yield from scaled(Mf, "memg", r_mem, tr, mp, state["bx_done"])
        state["mem_done"] = mp.tok[15]

    def s5_all():
        yield from s5_setup()
        yield from s5_main()
        yield from s5_gelu()

    TWO_PI = 2 * math.pi
    c1 = 6.28125
    c2 = float(np.float32(math.floor((TWO_PI - c1) * 2 ** 20) / 2 ** 20))
    c3 = float(np.float32(TWO_PI - c1 - c2))

    def reduce_angle(x, t, w):
        k = TS(t, x, 1 / TWO_PI, MAGIC, ALU.mult, ALU.add, w)
        k = TS(t, t, -MAGIC, None, ALU.add, None, k)
        yield
        for c in (c1, c2, c3):
            k = STT(x, t, -c, x, ALU.mult, ALU.add, k)
        yield
        return k

    def vexp(dst, x, t1, t2, w):
        k = TS(x, x, 88.7, -103.9, ALU.min, ALU.max, w)
        k = TS(t1, x, 1 / math.log(2), MAGIC, ALU.mult, ALU.add, k)
        k = TS(t1, t1, -MAGIC, None, ALU.add, None, k)
        yield
        k = STT(x, t1, -0.693359375, x, ALU.mult, ALU.add, k)
        k = STT(x, t1, 2.12194440e-4, x, ALU.mult, ALU.add, k)
        k2 = TS(t2, t1, 0.5, MAGIC, ALU.mult, ALU.add)
        k = TS(dst, x, 1 / 5040, None, ALU.mult, None, k)
        k2 = TS(t2, t2, -MAGIC, None, ALU.add, None, k2)
        yield
        for i, c in enumerate((1 / 720, 1 / 120, 1 / 24, 1 / 6, 0.5, 1.0)):
            k = STT(dst, dst, c, x, ALU.add, ALU.mult, k)
            if i == 0:
                k2 = TT(t1, t1, t2, ALU.subtract, k2)
            if i == 3:
                yield
        k = TS(dst, dst, 1.0, None, ALU.add, None, k)
        yield
        for t in (t1, t2):
            k = TS(x.bitcast(I32), t, 127.0, 8388608.0, ALU.add, ALU.mult, k, k2)
            k = TT(dst, dst, x, ALU.mult, k)
        yield
        return k

    V = lambda i: sv[:, i, :]
    s5 = {}

    def s5_setup():
        w = [state["sq_done"], state["x_done"]]
        k = TS(V(0), cvs("ldt"), 1.0, None, ALU.mult, None, w, t_c)
        k = yield from vexp(V(1), V(0), V(2), V(3), k)
        yield
        k = TS(V(4), cvs("are"), -1e-4, None, ALU.min, None, k)
        k = TT(V(5), V(4), V(1), ALU.mult, k)
        k = TT(V(6), cvs("aim"), V(1), ALU.mult, k)
        k = yield from vexp(V(7), V(5), V(2), V(3), k)
        yield
        k = yield from reduce_angle(V(6), V(2), k)
        k = TS(V(8), V(6), 16.0, None, ALU.mult, None, k)
        k = yield from reduce_angle(V(8), V(2), k)
        yield
        an = ang.rearrange("p (s k n) -> p s k n", s=2, k=32)
        io = cvs("iota")[:, None, :].broadcast_to((128, 32, 16))
        k1 = TT(an[:, 0, :, :], V(8)[:, :, None].broadcast_to((128, 32, 16)), io, ALU.mult, k)
        k = TT(an[:, 1, :, :], V(6)[:, :, None].broadcast_to((128, 32, 16)), io, ALU.mult, k)
        k = yield from reduce_angle(ang, angt, [k, k1])
        yield
        k = TS(ang, ang, 3.1415925, -3.1415925, ALU.min, ALU.max, k)
        ks = A(tab[:, :, 1, :, :], an, ACT.Sin, k)
        k = STT(angt, ang, -1.0, ang, ALU.mult, ALU.min, k)
        k = TS(angt, angt, math.pi / 2, None, ALU.add, None, k)
        kc = A(tab[:, :, 0, :, :], angt.rearrange("p (s k n) -> p s k n", s=2, k=32), ACT.Sin, k)
        yield
        lbr, lbi, lr, li = V(9), V(10), V(4), cvs("aim")
        k1 = TT(lbr, V(7), tab[:, 1, 0, :, 1], ALU.mult, ks, kc)
        k2 = TT(lbi, V(7), tab[:, 1, 1, :, 1], ALU.mult)
        k3 = TT(V(11), lr, lr, ALU.mult)
        k4 = TT(V(12), li, li, ALU.mult)
        k1 = TS(lbr, lbr, -1.0, None, ALU.add, None, k1)
        k3 = TT(V(11), V(11), V(12), ALU.add, k3, k4)
        k3 = dve.do(lambda e, n: e.reciprocal(V(11), V(11)), k3)
        yield
        a1 = TT(V(13), lbr, lr, ALU.mult, k1)
        a2 = TT(V(14), lbi, li, ALU.mult, k2)
        a3 = TT(V(15), lbi, lr, ALU.mult)
        a4 = TT(V(16), lbr, li, ALU.mult)
        a1 = TT(V(13), V(13), V(14), ALU.add, a1, a2)
        a3 = TT(V(15), V(15), V(16), ALU.subtract, a3, a4)
        a1 = TT(V(13), V(13), V(11), ALU.mult, a1, k3)
        a3 = TT(V(15), V(15), V(11), ALU.mult, a3)
        yield
        cr = V(13)[:, :, None].broadcast_to((128, 32, 32))
        ci = V(15)[:, :, None].broadcast_to((128, 32, 32))
        while "bc" not in state:
            yield
        b1 = TT(ct[:, 0, :, :], Cs[:, 0, :, :], ci, ALU.mult, a3, state["bc"])
        yield
        b2 = TT(Cs[:, 0, :, :], Cs[:, 0, :, :], cr, ALU.mult, a1, b1)
        b3 = TT(ct[:, 1, :, :], Cs[:, 1, :, :], ci, ALU.mult)
        yield
        b4 = TT(Cs[:, 1, :, :], Cs[:, 1, :, :], cr, ALU.mult, b3)
        yield
        b5 = TT(Cs[:, 0, :, :], Cs[:, 0, :, :], ct[:, 1, :, :], ALU.subtract, b2, b3)
        yield
        b6 = STT(Cs[:, 1, :, :], Cs[:, 1, :, :], -1.0, ct[:, 0, :, :], ALU.mult, ALU.subtract, b4, b1)
        rk = TS(rr, V(7), 1.0, None, ALU.mult, None)
        s5["ready"] = [b5, b6, ks, kc, rk]
        s5["sv"] = [b5, b6, rk]
        state["s5_ready"] = True
        yield

    rr = cvs("ldt")

    av = {}
    u_tok = [None] * 8
    s5y = [None] * 8
    cs_free = [None, None]
    w_free = {"m": None, "n": None, "s": None, "p": None}

    def s5_tables(k):
        i = k % 2
        cs = wcs[i]

        def outer(dst, j, *w):
            d = dst.rearrange("p r (a b) -> p r a b", a=16)
            tok = []
            for r in range(2):
                x = tab[:, 0, r, k, :][:, :, None].broadcast_to((128, 16, 16))
                y = tab[:, 1, j, k, :][:, None, :].broadcast_to((128, 16, 16))
                tok.append(TT(d[:, r, :, :], x, y, ALU.mult, *w, q=pool))
            return tok

        p1 = outer(cs, 0, s5["ready"], cs_free[i])
        p2 = outer(wpt, 1, w_free["p"])
        pa = TT(cs[:, 0, :], cs[:, 0, :], wpt[:, 1, :], ALU.subtract, p1, p2, q=pool)
        pb = TT(cs[:, 1, :], cs[:, 1, :], wpt[:, 0, :], ALU.add, q=pool)
        w_free["p"] = [pa, pb]
        return [pa, pb]

    def s5_main():
        cy = None
        tk = s5_tables(0)
        for k in range(32):
            tt, q = k // 4, k % 4
            i = k % 2
            cs, sc = wcs[i], wsc
            bk = 4 + i

            def bu(e, n, tt=tt, q=q, bk=bk):
                for r in range(2):
                    ins = e.matmul(bank[bk][:, r * T:(r + 1) * T], Bs[32 * q:32 * q + 32, r, tt, :],
                                   uT[32 * q:32 * q + 32, tt, :], start=True, stop=True)
                return ins

            tb = pe.do(bu, u_tok[tt], state["bc"], bfree[bk])
            tk_now = tk
            if k < 31:
                tk = s5_tables(k + 1)
            yield
            cb = cs[:, 0:1, :].broadcast_to((128, 2, T))
            sb_ = cs[:, 1:2, :].broadcast_to((128, 2, T))
            bv = bank[bk].rearrange("p (r t) -> p r t", r=2)
            m1 = TT(wm1, bv, cb, ALU.mult, tb, tk_now, s5["ready"], w_free["m"])
            m2 = TT(wm2, bv, sb_, ALU.mult)
            bfree[bk] = [m1, m2]
            yield
            if cy:
                cy()
            v1 = TT(wm1[:, 0, :], wm1[:, 0, :], wm2[:, 1, :], ALU.add, m1, m2)
            v2 = TT(wm1[:, 1, :], wm1[:, 1, :], wm2[:, 0, :], ALU.subtract)
            rb = rr[:, k:k + 1].broadcast_to((128, T))
            sc1 = dve.do(lambda e, n, sc=sc, rb=rb: e.tensor_tensor_scan(sc[:, 0, :], rb, wm1[:, 0, :], 0.0, ALU.mult, ALU.add), v1, w_free["s"])
            sc2 = dve.do(lambda e, n, sc=sc, rb=rb: e.tensor_tensor_scan(sc[:, 1, :], rb, wm1[:, 1, :], 0.0, ALU.mult, ALU.add), v2)
            w_free["m"] = [sc1, sc2]
            yield
            n1 = TT(wn1, sc, cb, ALU.mult, sc1, sc2, w_free["n"])
            n2 = TT(wn2, sc, sb_, ALU.mult)
            yield
            w_free["s"] = [n1, n2]
            cs_free[i] = [n1, n2]
            n3 = TT(wn1[:, 0, :], wn1[:, 0, :], wn2[:, 1, :], ALU.subtract, n1, n2)
            n4 = TT(wn1[:, 1, :], wn1[:, 1, :], wn2[:, 0, :], ALU.add)
            yield

            def cy(k=k, q=q, tt=tt, n3=n3, n4=n4):
                def mm(e, n):
                    e.matmul(bank[6][32 * q:32 * q + 32, 0:T], Cs[:, 0, k, :], wn1[:, 0, :], start=True, stop=False)
                    return e.matmul(bank[6][32 * q:32 * q + 32, 0:T], Cs[:, 1, k, :], wn1[:, 1, :], start=False, stop=True)

                ty = pe.do(mm, n3, n4, bfree[6] if q == 0 else None)
                w_free["n"] = [ty]
                if q == 3:
                    s5y[tt] = STT(uT[:, tt, :], uT[:, tt, :], cv("d", tt), bank[6][:, 0:T], ALU.mult, ALU.add, ty)
                    bfree[6] = [s5y[tt]]
        cy()
        s5["work_done"] = [w_free["n"], w_free["p"], w_free["m"], w_free["s"]]

    gp = Pair(Yr[:, 0:16, :], 8)
    ya = Pair(Yr[:, 0:16, :], 8)
    yx = Pair(Yr[:, 16:32, :], 8)
    yb = Pair(Yr[:, 32:48, :], 8)

    def s5_gelu():
        while "ya_done" not in state:
            yield
        for t in range(8):
            y = uT[:, t, :]
            si, s, fr = scr.next()
            k = A(s, y, ACT.Square, s5y[t], fr)
            yield
            k = TS(s, s, 0.044715, 1.0, ALU.mult, ALU.add, k)
            k = TT(s, s, y, ALU.mult, k)
            yield
            k = A(s, s, ACT.Tanh, k, scale=math.sqrt(2 / math.pi))
            yield
            k = STT(y, s, 1.0, y, ALU.add, ALU.mult, k)
            scr.free[si] = [k]
            yield
            s5y[t] = split(y, gp, t, 1, [k, state["ya_done"]], scale=0.5)
            yield

    def gated(bk, done, src_tok, other, pair, t, war=None):
        si, s, fr = scr.next()
        k0, rd = comb(bk, done, s, fr)
        k1 = A(s, s, ACT.Silu, k0)
        k3 = TT(s, s, other, ALU.mult, k1, src_tok)
        ks = split(s.rearrange("p (o t) -> p o t", o=1), pair, t, 1, [k3, war])
        scr.free[si] = ks
        return rd, ks

    def ev_bx(t):
        def f(bk, done):
            state["want_rx"] = True
            while "rx" not in state:
                step()
            k, rd = comb(bk, done, uT[:, t, :])
            u_tok[t] = TT(uT[:, t, :], uT[:, t, :], r_x, ALU.mult, k, state["rx"])
            return rd
        return f

    sums = small[:, 0:4].rearrange("p (c g) -> p c g", c=2)
    stat = small[:, 4:16]

    def ev_av(g):
        def f(bks, done):
            r = []
            for c in range(2):
                r.append([A(vn[:, c, g * 512:(g + 1) * 512], bks[c], ACT.Copy, done, state["mem_done"],
                            accum_out=sums[:, c, g:g + 1])])
            av[g] = r
            return r
        return f

    def spatial():
        def bias():
            while "sg" not in state:
                yield
            tm = pool.do(lambda e, n: e.affine_select(out=sgw[:, :, :], in_=sgw[:, :, :], compare_op=ALU.is_ge, fill=0.0,
                                                      base=0, pattern=[[0, 8], [1, 128]], channel_multiplier=-1), state["sg"])
            lb = TS(cvs("glnb"), cvs("glnb"), 2048.0, None, ALU.mult, None, t_c)
            yield
            tb = [None] * 8
            for h in range(2):
                ks = pe.do(lambda e, n, h=h: e.matmul(bank[7], ones, sgw[:, 4 * h:4 * h + 4, :], start=True, stop=True),
                           tm, t_ones, bfree[7])
                yield
                for g in range(4 * h, 4 * h + 4):
                    tb[g] = STT(sgb[:, g, :], bank[7][:, (g % 4) * 128:(g % 4) * 128 + 128], cv("glnb", g), sgb[:, g, :],
                                ALU.mult, ALU.add, ks, lb, state["sg"])
                bfree[7] = [tb[4 * h + 3]]
                yield
            state["sg_bias"] = [tm, tb]

        def gen():
            while 1 not in av or "sg_bias" not in state:
                yield
            tm, tb = state["sg_bias"]
            st = [stat[:, 4 * c:4 * c + 4] for c in range(2)]
            k = []
            for c in range(2):
                k.append(TT(st[c][:, 0:1], sums[:, c, 0:1], sums[:, c, 1:2], ALU.add, av[0], av[1]))
            for c in range(2):
                k[c] = TS(st[c][:, 0:1], st[c][:, 0:1], -1.0 / 1024, None, ALU.mult, None, k[c])
            yield
            zf = zb.rearrange("p n t -> p (n t)")
            kv2 = [None, None]
            for c in range(2):
                k[c] = A(vn[:, c, :], vn[:, c, :], ACT.Identity, k[c], bias=st[c][:, 0:1])
                yield
                kv2[c] = A(zf[:, c * 1024:(c + 1) * 1024], vn[:, c, :], ACT.Square, k[c], accum_out=st[c][:, 1:2])
                yield
            for c in range(2):
                k[c] = TS(st[c][:, 1:2], st[c][:, 1:2], 1.0 / 1024, 1e-6, ALU.mult, ALU.add, kv2[c])
            yield
            for c in range(2):
                k[c] = A(st[c][:, 1:2], st[c][:, 1:2], ACT.Sqrt, k[c])
            yield
            for c in range(2):
                k[c] = dve.do(lambda e, n, c=c: e.reciprocal(st[c][:, 2:3], st[c][:, 1:2]), k[c])
            vt = []
            for c in range(2):
                vt.append(A(vn[:, c, :], vn[:, c, :], ACT.Copy, k[c], scale=st[c][:, 2:3]))
                yield
            for g0 in range(0, 8, 2):

                def z(e, n, g0=g0):
                    for g in (g0, g0 + 1):
                        for c in range(2):
                            o = 256 * (g - g0) + 128 * c
                            ins = e.matmul(bank[7][:, o:o + 128], vn[:, c, g * 128:g * 128 + 128], sgw[:, g, :],
                                           start=True, stop=True)
                    return ins

                tz = pe.do(z, vt, tm, bfree[7])
                yield
                for g in (g0, g0 + 1):
                    o = 256 * (g - g0)
                    k = STT(zb[:, g, :].rearrange("p (c t) -> p c t", c=2),
                            bank[7][:, o:o + 256].rearrange("p (c t) -> p c t", c=2), cv("glng", g),
                            sgb[:, g:g + 1, :].broadcast_to((128, 2, 128)), ALU.mult, ALU.add, tz, kv2, tb[g])
                    av["z", g] = k
                bfree[7] = [k]
                yield
            state["sg_done"] = [k, tz]
        background.append(bias())
        background.append(gen())

    def ev_au(t):
        def f(bk, done):
            si, s, fr = scr.next()
            k, rd = comb(bk, done, s, fr)
            k = TT(zb[:, t, :], zb[:, t, :], s, ALU.mult, k, av["z", t])
            scr.free[si] = [k]
            av["zu", t] = k
            return rd
        return f

    def ev_ag(t):
        def f(bk, done):
            r, ks = gated(bk, done, av["zu", t], zb[:, t, :], ya, t, state["kv_done"])
            state["zb_done"] = ks
            return r
        return f

    kv = {"K": [], "V": [], "q": []}

    def ev_k(t):
        def f(bk, done):
            k, rd = comb(bk, done, KT[:, t, :], state["x_done"], s5["sv"])
            kv["K"].append(k)
            return rd
        return f

    def ev_v(g):
        def f(bks, done):
            r = [[A(Vn[:, m, g * 512:(g + 1) * 512], bks[m], ACT.Copy, done, state["sg_done"])] for m in range(2)]
            kv["V"] += r
            return r
        return f

    def ev_q(t):
        def f(bk, done):
            k, rd = comb(bk, done, qT[:, t, :], state["x_done"], scale=1.0 / 16)
            kv["q"].append(k)
            return rd
        return f

    o_tok = [None] * 8

    def attention():
        def gen():
            pb_free = [None, None]
            pt_free = state["sg_done"]
            for h in range(4):
                pt = []
                for s in range(2):
                    bk = 7

                    def sc(e, n, h=h, s=s):
                        for d in range(2):
                            ins = e.matmul(bank[7][:, 0:T], qT[:, 2 * h + d, s * 128:s * 128 + 128], KT[:, 2 * h + d, :],
                                           start=d == 0, stop=d == 1)
                        return ins

                    ts_ = pe.do(sc, kv["K"], kv["q"], bfree[7])
                    P = Pb[s]
                    mx = stat[:, 4 * s:4 * s + 1]
                    sm = stat[:, 4 * s + 1:4 * s + 2]
                    yield
                    k = dve.do(lambda e, n, mx=mx: e.reduce_max(mx, bank[7][:, 0:T], AX), ts_, pb_free[s])
                    k = TS(mx, mx, -1.0, None, ALU.mult, None, k)
                    k = A(P, bank[7][:, 0:T], ACT.Exp, k, bias=mx, accum_out=sm)
                    bfree[7] = [k]
                    yield
                    k = dve.do(lambda e, n, sm=sm: e.reciprocal(sm, sm), k)
                    k = TS(P, P, sm, None, ALU.mult, None, k)

                    def tr(e, n, P=P):
                        for m in range(2):
                            ins = e.transpose(bank[7][:, 256 + m * 128:256 + m * 128 + 128], P[:, m * 128:m * 128 + 128], ident)
                        return ins

                    yield
                    k = pe.do(tr, k, t_id, bfree[7])
                    pb_free[s] = [k]
                    k = A(pT[:, :, s * 128:s * 128 + 128], bank[7][:, 256:512].rearrange("p (m t) -> p m t", m=2),
                          ACT.Copy, k, pt_free)
                    bfree[7] = [k]
                    pt.append(k)
                    yield
                last = []
                for d in range(2):
                    t = 2 * h + d

                    def pv(e, n, t=t):
                        for m in range(2):
                            ins = e.matmul(bank[7][:, 0:T], Vn[:, m, t * 128:t * 128 + 128], pT[:, m, :],
                                           start=m == 0, stop=m == 1)
                        return ins

                    k = pe.do(pv, pt, kv["V"], bfree[7])
                    last.append(k)
                    k = A(qT[:, t, :], bank[7][:, 0:T], ACT.Copy, k)
                    bfree[7] = [k]
                    o_tok[t] = k
                    yield
                pt_free = last
            state["att_done"] = [last, pb_free, k]
        background.insert(0, gen())

    def ev_xg(t):
        def f(bk, done):
            r, ks = gated(bk, done, o_tok[t], qT[:, t, :], yx, t, state["att_done"])
            state["xg_done"] = ks
            return r
        return f

    gate = {}
    mg_tok = [None] * 16

    def ev_gate(t):
        def f(bk, done):
            si, s, fr = scr.next()
            k, rd = comb(bk, done, s, fr)
            gate[t] = (si, s, A(s, s, ACT.Tanh, k, scale=0.5))
            return rd
        return f

    def ev_gate_kept(t):
        def f(bk, done):
            s = Xf[:, t, :]
            k, rd = comb(bk, done, s, state["xg_done"], state["att_done"])
            gate[t] = (None, s, A(s, s, ACT.Tanh, k, scale=0.5))
            return rd
        return f

    def ev_branch(t, first):
        def f(bk, done):
            si, s, kg = gate[t]
            if first:
                k, rd = comb(bk, done, Mf[:, t, :], state["zb_done"])
                k = STT(Mf[:, t, :], s, 1.0, Mf[:, t, :], ALU.add, ALU.mult, k, kg)
                mg_tok[t] = k
                scr.free[si] = [k]
                return rd
            si2, s2, fr = scr.next()
            k, rd = comb(bk, done, s2, fr)
            k = STT(s2, s, 1.0, s2, ALU.add, ALU.mult, k, kg)
            k2 = TT(Mf[:, t, :], Mf[:, t, :], s2, ALU.add, k, mg_tok[t])
            if si is not None:
                scr.free[si] = [k]
            scr.free[si2] = [k2]
            mg_tok[t] = k2
            return rd
        return f

    mgp = Pair(Yr[:, 0:32, :], 16)

    def ev_branch_last(t):
        def f(bk, done):
            r = ev_branch(t, False)(bk, done)

            def later():
                yield
                split(Mf[:, t:t + 1, :], mgp, t, 1, [mg_tok[t], state["yx_done"], state["glu_done"]], scale=0.5)
            background.append(later())
            return r
        return f

    def ev_glu(t):
        def f(bk, done):
            si, s, fr = scr.next()
            k0, rd = comb(bk, done, s, fr)
            k = TS(s, s, cv("glub", t), 0.5, ALU.add, ALU.mult, k0)
            k1 = A(s, s, ACT.Tanh, k)
            k2 = STT(uT[:, t, :], s, 1.0, uT[:, t, :], ALU.add, ALU.mult, k1, s5y[t])
            scr.free[si] = [k2]
            av["glu", t] = k2
            return rd
        return f

    def ev_bg(t):
        def f(bk, done):
            si, s, fr = scr.next()
            k0, rd = comb(bk, done, s, fr)
            k1 = A(s, s, ACT.Silu, k0)
            k3 = TT(s, s, uT[:, t, :], ALU.mult, k1, av["glu", t])
            ks = split(s.rearrange("p (o t) -> p o t", o=1), yb, t, 1, [k3, s5["work_done"]], scale=0.25)
            scr.free[si] = ks
            return rd
        return f

    W = a
    def call(fn):
        jobs.append(fn)

    def ensure(*keys):
        def f():
            while not all(k in state for k in keys):
                step()
        return f

    def mark_pe(name):
        def f():
            state[name] = [(pe.sem, pe.n)]
        return f

    group(*[("W", W["w_bx"], t, 2, hp0, ev_bx(t)) for t in range(4)])
    for t in range(4, 8):
        job("W", W["w_bx"], t, 2, hp0, ev_bx(t))
    pool_chunks.update(range(4, 32, 2))
    call(mark_pe("bx_done"))
    call(ensure("x_done"))
    for t in range(8):
        job("W", W["w_q"], t, 2, hp, ev_q(t))
    call(spatial)
    call(ensure("mem_done"))
    for g in range(2):
        job("M", W["w_av"], g, 8, hp, ev_av(g))
    call(ensure("s5_ready"))
    for t in range(8):
        job("W", W["w_k"], t, 2, mp, ev_k(t))
    call(ensure("sg_done"))
    for g in range(2):
        job("M", W["w_v"], g, 8, mp, ev_v(g))
    call(mark_pe("kv_done"))
    for t in range(8):
        job("W", W["w_au"], t, 2, hp, ev_au(t))
        job("W", W["w_ag"], t, 2, hp, ev_ag(t))
    call(attention)
    for t in range(16):
        job("W", W["w_g0"], t, 2, hp, ev_gate(t))
        job("W", W["w_b0"], t, 1, ya, ev_branch(t, True))
    call(mark_pe("ya_done"))
    call(ensure("att_done"))
    for t in range(8):
        job("W", W["w_xg"], t, 2, hp, ev_xg(t))
    for t in range(16):
        job("W", W["w_g2"], t, 2, hp, ev_gate(t))
        job("W", W["w_b2"], t, 1, yx, ev_branch(t, False))
    call(mark_pe("yx_done"))
    for t in range(12):
        job("W", W["w_g1"], t, 2, hp, ev_gate_kept(t))
    call(drain)
    for t in range(12, 14):
        job("W", W["w_g1"], t, 2, hp, ev_gate_kept(t))
    for t in range(8):
        job("W", W["w_glu"], t, 1, gp, ev_glu(t))

    def after_glu():
        state["glu_done"] = [(pe.sem, pe.n)]
    call(after_glu)
    for t in range(8):
        job("W", W["w_bg"], t, 2, hp, ev_bg(t))
    for t in range(14, 16):
        job("W", W["w_g1"], t, 2, hp, ev_gate_kept(t))
    for t in range(16):
        job("W", W["w_b1"], t, 1, yb, ev_branch_last(t))

    acc = {}

    def square_sum(src, w, key, q=None):
        si, s, fr = scr2.next()
        k = A(s, src, ACT.Square, w, fr)
        return add_to(key, si, s, k)

    def add_to(key, si, s, k):
        dst = (keep + extra)[key[1]]
        if acc.get(key) is None:
            k2 = TS(dst, s, 1.0, None, ALU.mult, None, k, acc.get(("free", key[1])))
        else:
            k2 = TT(dst, dst, s, ALU.add, k, acc[key])
        acc[key] = k2
        scr2.free[si] = [k2]
        return k

    f_tok = [None] * 16

    def ev_out(t):
        def f(bk, done):
            if t == 0:
                act.plain(lambda e, n: e.preload_act_table(ACT.Sqrt))
            si, s, fr = scr2.next()
            k, rd = comb(bk, done, s, fr, state["F_free"])

            def later():
                yield
                k2 = square_sum(s, k, ("post", 0))
                f_tok[t] = A(F0[:, t, :], s, ACT.Copy, k, state["F_free"], scale=cv("post", t))
                scr2.free[si] = [f_tok[t], k2]
                yield
                square_sum(F0[:, t, :], f_tok[t], ("ff", 4))
                sj, s2, fr = scr2.next()
                kx = TT(s2, Xf[:, t, :], F0[:, t, :], ALU.mult, f_tok[t], t_x2, fr)
                add_to(("xf", 2), sj, s2, kx)
            background.append(later())
            return rd
        return f

    t_x2 = []

    def reload_x():
        drain()
        state["F_free"] = [yb.tok, state["att_done"], s5["work_done"]]
        for i in range(4):
            t_x2.append(load(sp, f"xagain{i}", [(Xf[:, 4 * i:4 * i + 4, :], a["xT"][:, 4 * i:4 * i + 4, :])],
                             mg_tok[4 * i:4 * i + 4]))
    call(reload_x)

    def x_squares():
        def gen():
            for t in range(16):
                square_sum(Xf[:, t, :], t_x2[t // 4], ("xx", 5))
                yield
        background.append(gen())

    group(*[("W", W["w_out"], t, 2, mgp, ev_out(t)) for t in range(4)])
    call(x_squares)
    for t in range(4, 16):
        if t == 15:
            call(lambda: state.update(late=True))
        job("W", W["w_out"], t, 2, mgp, ev_out(t))

    x_tok = [None] * 16
    h1 = Pair(Hr, 16)
    one = lambda ap: ap.rearrange("p (o t) -> p o t", o=1)

    def post():
        drain()
        r, r2, sxf, sff, sxx = keep[1], keep[3], keep[2], extra[0], extra[1]
        tr = rstd_of(keep[0], r, 1e-6, acc["post", 0], None)
        war = [(pe.sem, pe.n), mg_tok, mgp.tok]
        k = TT(sff, sff, r, ALU.mult, tr, acc["ff", 4])
        k = STT(sff, sxf, 2.0, sff, ALU.mult, ALU.add, k, acc["xf", 2])

        def x1a(t0, nt):
            f = F0[:, t0:t0 + nt, :]
            return TT(f, f, one(r).broadcast_to((128, nt, T)), ALU.mult, tr, f_tok[t0:t0 + nt])

        def x1(t0, nt, k=None):
            f, x = F0[:, t0:t0 + nt, :], Xf[:, t0:t0 + nt, :]
            k = TT(x, x, f, ALU.add, k or x1a(t0, nt), t_x2)
            for t in range(t0, t0 + nt):
                x_tok[t] = k

        k = TT(sff, sff, r, ALU.mult, k)
        k = TT(sxx, sxx, sff, ALU.add, k, acc["xx", 5])
        tm = mean_of(sxx, k)
        kf = x1a(0, 4)
        te = TS(r2, bank[7][:, 0:T], 0.0, 1e-5, ALU.max, ALU.add, tm)
        bfree[7] = [te]
        x1(0, 4, kf)
        ts_ = A(r2, r2, ACT.Sqrt, te)
        tr2 = dve.do(lambda e, n: e.reciprocal(r2, r2), ts_)
        act.plain(lambda e, n: e.preload_act_table(ACT.Tanh))
        state["late"] = False
        split_chunk()
        rest = None
        for t in range(16):
            if t in (2, 6, 10):
                x1(t + 2, 4)
            k = STT(Mf[:, t, :], Xf[:, t, :], cv("mix", t), r2, ALU.mult, ALU.mult, tr2, x_tok[t], war)
            late, rest = rest, split_later(Mf[:, t:t + 1, :], h1, t, 1, [k, war])
            if late:
                late()
        rest()
        state["h1"] = [tm, h1.tok[15]]
    call(post)

    hb = small[:, 16:32]
    pads = Slots(upad)
    conv_in = {}
    c_tok = [None] * 16

    def ev_a(t):
        def f(bk, done):
            si, s, fr = scr2.next()
            conv_in[t] = (si, s, A(s, bk, ACT.Identity, done, fr, bias=cv("bpw1", t)))
            return [conv_in[t][2]]
        return f

    def ev_gt(t):
        def f(bk, done):
            if t == 0:
                state["hb"] = TS(hb, cvs("bpw1")[:, 16:32], 0.5, None, ALU.mult, None)
            si, s, fr = scr2.next()
            kt = A(s, bk, ACT.Tanh, done, fr, state["hb"], scale=0.5, bias=hb[:, t:t + 1])
            sa, sap, ka = conv_in[t]
            while 4 <= t < 14 and c_tok[t - 4] is None:
                step()
            while not any(f is not None for f in pads.free):
                step()
            pi, pad, pf = pads.next()
            if t < 4:
                z1 = dve.do(lambda e, n: e.memset(pad, 0.0), state["h1"], x_tok[15])
            else:
                z1 = None
            ku = STT(pad[:, 15:271], s, 1.0, sap, ALU.add, ALU.mult, kt, ka, pf, z1)
            scr2.free[si] = [ku]
            scr2.free[sa] = [ku]
            conv_in["u", t] = (pi, pad, ku)
            if t >= 14:
                uh, ul = ub[t - 14]
                kh = A(uh[:, 0:286], pad, ACT.Copy, ku)
                kl = TT(ul[:, 0:286], pad, uh[:, 0:286].bitcast(F32), ALU.subtract, kh)
                pads.free[pi] = [kh, kl]
                conv_in["ub", t] = [kh, kl]
            return [kt]
        return f

    def conv():
        now, nxt, n = {}, 0, 0
        state["taps"] = 0
        while nxt < 14 or now:
            for i in range(2):
                if i not in now and ("u", nxt) in conv_in and nxt < 14:
                    now[i] = [nxt, 0, conv_in["u", nxt]]
                    nxt += 1
            if not now:
                yield
                continue
            for i in sorted(now):
                t, j, (pi, pad, k) = now[i]
                ac = bank[4 + i][:, 0:T]
                wj = cst[:, C_OFF["wdw"][0] + t * 31 + j:C_OFF["wdw"][0] + t * 31 + j + 1]
                if j == 0:
                    k = TS(ac, pad[:, j:j + T], wj, cv("bdw", t), ALU.mult, ALU.add, k, state["h1"], state["wdw"],
                           bfree[4 + i])
                else:
                    k = STT(ac if j < 30 else Mf[:, t, :], pad[:, j:j + T], wj, ac, ALU.mult, ALU.add, k)
                now[i] = [t, j + 1, (pi, pad, k)]
                if j == 30:
                    pads.free[pi] = [k]
                    c_tok[t] = k
                    bfree[4 + i] = [k]
                    del now[i]
                n += 1
                state["taps"] += 1
            if n >= (6 if c_tok[10] is None else 3) or state["taps"] == 14 * 31 - 18:
                n = 0
                yield

    def diagonals():
        w = cst[:, C_OFF["wdw"][0] + 14 * 31:C_OFF["wdw"][0] + 16 * 31]
        kh = A(w62[0], w, ACT.Copy, state["wdw"], state["F1_free"])
        kl = TT(w62[1], w, w62[0].bitcast(F32), ALU.subtract, kh)
        yield
        tok = [None, None]
        for i in range(2):
            for j in range(31):
                c = i * 31 + j
                A(dg[i][0][:, j, :], ident, ACT.Copy, t_id, state["F1_free"], scale=w[:, c:c + 1])
                tok[i] = A(dg[i][1][:, j, :], ident, ACT.Copy, kl, scale=w62[1][:, c:c + 1])
                if j % 4 != 3:
                    yield
        state["dg"] = tok

    def conv_pe():
        while "dg" not in state:
            step()
        for i, bk in enumerate((6, 0)):
            t = 14 + i

            def taps(e, n, i=i, bk=bk):
                for j in range(31):
                    dh, dl = dg[i][0][:, j, :], dg[i][1][:, j, :]
                    uh, ul = (x[:, j:j + T] for x in ub[i])
                    e.matmul(bank[bk][:, 0:T], dh, uh, start=j == 0, stop=False)
                    e.matmul(bank[bk][:, 0:T], dh, ul, start=False, stop=False)
                    ins = e.matmul(bank[bk][:, 0:T], dl, uh, start=False, stop=j == 30)
                return ins

            k = pe.do(taps, state["dg"][i], conv_in["ub", t], bfree[bk])
            state["conv_pe"] = k
            c_tok[t] = A(Mf[:, t, :], bank[bk][:, 0:T], ACT.Identity, k, state["h1"], bias=cv("bdw", t))
            bfree[bk] = [c_tok[t]]

    def halve_w():
        state["F1_free"] = [(pe.sem, pe.n), (dve.sem, dve.n), (act.sem, act.n)]
        state["wdw"] = TS(cvs("wdw"), cvs("wdw"), 0.5, None, ALU.mult, None, t_c)
        background.append(conv())
        background.append(diagonals())
        background.append(pivot())
    call(halve_w)
    c_p1 = len(chunks)
    group(*[("T", W["w_p1"], 16 * i + t, 2, h1, (ev_gt if i else ev_a)(t)) for t in range(2) for i in range(2)])
    for t in range(2, 16):
        job("T", W["w_p1"], t, 2, h1, ev_a(t))
        job("T", W["w_p1"], 16 + t, 2, h1, ev_gt(t))
    c_end = len(chunks)
    pool_chunks.update(range(c_p1, c_end + 4))
    cp = Pair(Yr[:, 0:32, :], 16)

    def until(i):
        while c_tok[i] is None:
            step()

    mA, m1, m2, rs = keep
    kc, ks = [None] * 16, [None] * 16

    def msum(bk, src, ts, waits, first=True, last=True):
        waits = list(waits)
        def f(e, n):
            for t in ts:
                for x in flat(waits[t]):
                    n(x)
                ins = e.matmul(bank[bk][:, 0:T], ones, src[:, t, :], start=first and t == ts[0], stop=last and t == ts[-1])
            return ins
        return pe.do(f, t_ones, bfree[bk] if first else None)

    def centre(t0, nt):
        m = Mf[:, t0:t0 + nt, :]
        k = TT(m, m, one(mA).broadcast_to((128, nt, T)), ALU.subtract, state["mA"], c_tok[t0:t0 + nt])
        for t in range(t0, t0 + nt):
            kc[t] = k

    def square(t0, nt):
        k = A(F1[:, t0:t0 + nt, :], Mf[:, t0:t0 + nt, :], ACT.Square, kc[t0:t0 + nt], state["p1_done"])
        for t in range(t0, t0 + nt):
            ks[t] = k

    def pivot():
        while c_tok[7] is None:
            yield
        yield
        yield
        km = msum(7, Mf, range(8), c_tok)
        km = A(mA, bank[7][:, 0:T], ACT.Copy, km, scale=2.0)
        bfree[7] = [km]
        state["mA"] = km
        yield
        for t0 in (0, 4, 8):
            while c_tok[t0 + 3] is None:
                yield
            centre(t0, 4)
            yield

    def ln2():
        state["p1_done"] = (pe.sem, pe.n)
        conv_pe()
        act.plain(lambda e, n: e.preload_act_table(ACT.Sqrt))
        while kc[11] is None:
            step()
        for t0 in (0, 4, 8):
            square(t0, 4)
        msum(6, F1, range(12), ks, last=False)
        msum(7, Mf, range(8, 12), kc, last=False)
        while state["taps"] < 14 * 31 - 18:
            step()
        centre(14, 2)
        square(14, 2)
        msum(7, Mf, (14, 15), kc, first=False, last=False)
        msum(6, F1, (14, 15), ks, first=False, last=False)
        until(13)
        centre(12, 2)
        square(12, 2)
        k1 = msum(7, Mf, (12, 13), kc, first=False)
        k2 = msum(6, F1, (12, 13), ks, first=False)
        k1 = A(m1, bank[7][:, 0:T], ACT.Copy, k1)
        bfree[7] = [k1]
        k = TT(m2, m1, m1, ALU.mult, k1)
        kd = {}
        rest = None

        def less(t0, nt):
            m = Mf[:, t0:t0 + nt, :]
            kd[t0] = TT(m, m, one(m1).broadcast_to((128, nt, T)), ALU.subtract, k1, kc[t0:t0 + nt])
        less(0, 4)
        k = STT(m2, bank[6][:, 0:T], 1e-5, m2, ALU.add, ALU.subtract, k2, k)
        bfree[6] = [k]
        k = A(m2, m2, ACT.Sqrt, k)
        k = dve.do(lambda e, n: e.reciprocal(rs, m2), k)
        act.plain(lambda e, n: e.preload_act_table(ACT.Silu))
        for t0 in range(0, 16, 2):
            m = Mf[:, t0:t0 + 2, :]
            if t0 in (2, 6, 10):
                less(t0 + 2, 4)
            ka = TT(m, m, one(rs).broadcast_to((128, 2, T)), ALU.mult, kd[t0 // 4 * 4], k)
            kk = [A(Mf[:, t, :], Mf[:, t, :], ACT.Silu, ka, scale=cv("lng", t), bias=cv("lnb", t))
                  for t in (t0, t0 + 1)]
            late, rest = rest, split_later(m, cp, t0, 2, [kk, state["conv_pe"]])
            if late:
                late()
        rest()
        state["cp"] = cp.tok[15]
    call(ln2)

    h2 = Pair(Hr, 16)

    def ev_p2(t):
        def f(bk, done):
            k = STT(Xf[:, t, :], bk[:, 0:T], cv("bpw2", t), Xf[:, t, :], ALU.add, ALU.add, done, x_tok[t])
            k = TT(Xf[:, t, :], Xf[:, t, :], bk[:, T:2 * T], ALU.add, k)
            x_tok[t] = k
            ka = A(h2.hi[:, t, :], Xf[:, t, :], ACT.Copy, k, scale=cv("ffn", t))
            kd = STT(h2.lo[:, t, :], Xf[:, t, :], cv("ffn", t), h2.hi[:, t, :].bitcast(F32), ALU.mult, ALU.subtract, ka)
            h2.tok[t] = [ka, kd]
            square_sum(Xf[:, t, :], k, ("ffn", 0))
            if t == 0:
                act.plain(lambda e, n: e.preload_act_table(ACT.Sqrt))
            return [k]
        return f

    group(*[("W", W["w_p2"], t, 2, cp, ev_p2(t)) for t in range(4)])
    for t in range(4, 16):
        job("W", W["w_p2"], t, 2, cp, ev_p2(t))

    def pre_ffn():
        state["r_ffn"] = rstd_of(keep[0], keep[1], 1e-5, acc["ffn", 0], None)

    hid = [Pair(Yr[:, 0:32, :], 16) for _ in range(4)]

    def ev_up(q, t):
        def f(bk, done):
            si, s, fr = scr2.next()
            k, rd = comb(bk, done, s, fr)
            k = TT(s, s, keep[1], ALU.mult, k, state["r_ffn"])
            k2 = STT(s, s, 0.0, s, ALU.max, ALU.mult, k)
            ks = split(s.rearrange("p (o t) -> p o t", o=1), hid[q], t, 1, [k2, state["war_hid"]])
            scr2.free[si] = ks
            return rd
        return f

    def ev_dn(q, t):
        def f(bk, done):
            k = TT(Xf[:, t, :], Xf[:, t, :], bk[:, 0:T], ALU.add, done, x_tok[t])
            k = TT(Xf[:, t, :], Xf[:, t, :], bk[:, T:2 * T], ALU.add, k)
            x_tok[t] = k
            if q == 3:
                square_sum(Xf[:, t, :], k, ("fin", 2))
            return [k]
        return f

    def mark():
        state["war_hid"] = [(pe.sem, pe.n)]

    for q in range(4):
        call(mark)
        if q == 0:
            group(*[("W", W["w_up"], t, 2, h2, ev_up(0, t)) for t in range(4)], hooks={2: pre_ffn})
        for t in range(0 if q else 4, 16):
            job("W", W["w_up"], 16 * q + t, 2, h2, ev_up(q, t))
        for t in range(16):
            job("W", W["w_dn"], 16 * q + t, 2, hid[q], ev_dn(q, t))

    s_out = sem("s_out")

    def finish():
        tr = rstd_of(keep[2], keep[3], 1e-5, acc["fin", 2], None)
        for i in range(4):
            for t in range(4 * i, 4 * i + 4):
                k = STT(Xf[:, t, :], Xf[:, t, :], cv("fin", t), keep[3], ALU.mult, ALU.mult, tr, x_tok[t])
            tok = sp.dma(lambda e, n, i=i: e.dma_start(out[:, 4 * i:4 * i + 4, :], Xf[:, 4 * i:4 * i + 4, :]),
                         s_out, 16 * (i + 1), k)
        sp.only_wait(tok)
    call(finish)

    state["declared"] = True
    start_x()
    background.append(early())
    background.append(more_loads())
    run_jobs()
    drain()

    with nc.Block() as block:
        @block.sync
        def _(e):
            sp.emit(e)

        @block.gpsimd
        def _(e):
            pool.emit(e)

        @block.scalar
        def _(e):
            act.emit(e)

        @block.vector
        def _(e):
            dve.emit(e)

        @block.tensor
        def _(e):
            pe.emit(e)


def kernel(**x):
    import concourse.bacc as bacc
    from concourse.bass_utils import run_bass_kernel_spmd

    f = np.float32

    def cols(v):
        return np.asarray(v).reshape(-1, 128).T

    def tilesT(w):
        k, n = w.shape
        return np.ascontiguousarray(w.reshape(k // 1024, 8, 128, n // 128, 128).transpose(3, 0, 2, 1, 4)
                                    .reshape(n // 128, k // 1024, 128, 1024))

    def tilesM(w):
        k, n = w.shape
        return np.ascontiguousarray(w.reshape(k // 256, 2, 128, n // 512, 512).transpose(3, 0, 2, 1, 4)
                                    .reshape(n // 512, k // 256, 128, 1024))

    def actT(v):
        return np.ascontiguousarray(v[0].reshape(256, 16, 128).transpose(2, 1, 0))

    x = {k: np.asarray(v) for k, v in x.items()}
    pg = lambda v: v.reshape(32, 2, 64).transpose(1, 2, 0).reshape(128, 32)
    ldt = np.ascontiguousarray(np.broadcast_to(x["ssm_log_dt"][0][:, None], (64, 64)))
    wdw = x["conv_w_dw_2"][0].reshape(31, 16, 128).transpose(2, 1, 0).reshape(128, 496)
    parts = {
        "pre": cols(x["pre_norm_g"][0]), "memg": cols(x["mem_norm_g"][0]), "post": cols(x["post_norm_g"][0]),
        "glub": cols(x["glu_b"][0]), "d": cols(x["ssm_d"][0]), "mix": cols(x["norm_mix_g_2"][0]),
        "ffn": cols(x["norm_ffn_g_2"][0]), "fin": cols(x["final_norm_g_2"]), "bpw1": cols(x["conv_b_pw1_2"][0]),
        "bdw": cols(x["conv_b_dw_2"][0]), "lng": cols(x["conv_ln_g_2"][0]), "lnb": cols(x["conv_ln_b_2"][0]),
        "bpw2": cols(x["conv_b_pw2_2"][0]), "wdw": wdw, "glng": cols(x["sg_ln_g"][0]), "glnb": cols(x["sg_ln_b"][0]), "are": pg(x["ssm_a_re"][0]), "aim": pg(x["ssm_a_im"][0]),
        "ldt": pg(ldt), "iota": np.ascontiguousarray(np.broadcast_to(np.arange(16, dtype=f), (128, 16))),
    }
    cst = np.ascontiguousarray(np.concatenate([parts[k] for k in C_OFF], axis=1))
    BT = np.zeros((128, 2, 8, 128), f)
    CT = np.zeros((128, 2, 32, 32), f)
    for r, (bn, cn) in enumerate((("ssm_b_re", "ssm_c_re"), ("ssm_b_im", "ssm_c_im"))):
        b = x[bn][0].reshape(8, 4, 2, 64, 16)
        c = x[cn][0].reshape(32, 2, 16, 64)
        for g in range(2):
            for q in range(4):
                BT[32 * q + 16 * g:32 * q + 16 * g + 16, r, :, 64 * g:64 * g + 64] = b[:, q, g].transpose(2, 0, 1)
            CT[64 * g:64 * g + 64, r, :, 16 * g:16 * g + 16] = c[:, g].transpose(2, 0, 1)
    w_in = x["w_in"][0]
    seg = lambda i: w_in[:, 1024 * i:1024 * (i + 1)]
    gts = lambda i: w_in[:, 7168 + 2048 * i:7168 + 2048 * (i + 1)]
    wd = x["ffn_w_down_2"][0]
    arrays = {
        "xT": actT(x["x"]), "memT": actT(x["mem"]), "cst": cst, "BT": BT, "CT": CT,
        "sgw": np.ascontiguousarray(x["sg_w"][0].transpose(2, 0, 1)),
        "sgb": np.ascontiguousarray(np.broadcast_to(x["sg_b"][0], (128, 8, 128))),
        "w_au": tilesT(seg(0)), "w_av": tilesM(seg(1)), "w_ag": tilesT(seg(2)), "w_bx": tilesT(seg(3)),
        "w_bg": tilesT(seg(4)), "w_q": tilesT(seg(5)), "w_xg": tilesT(seg(6)),
        "w_g0": tilesT(gts(0)), "w_g1": tilesT(gts(1)), "w_g2": tilesT(gts(2)),
        "w_k": tilesT(x["xa_wk"][0]), "w_v": tilesM(x["xa_wv"][0]), "w_glu": tilesT(x["glu_w"][0]),
        "w_b0": tilesT(x["w_branch"][0, 0]), "w_b1": tilesT(x["w_branch"][0, 1]), "w_b2": tilesT(x["w_branch"][0, 2]),
        "w_out": tilesT(x["w_out"][0]), "w_p1": tilesT(x["conv_w_pw1_2"][0]), "w_p2": tilesT(x["conv_w_pw2_2"][0]),
        "w_up": tilesT(x["ffn_w_up_2"][0]),
        "w_dn": np.concatenate([tilesT(wd[2048 * i:2048 * (i + 1)]) for i in range(4)]),
    }
    nc = bacc.Bacc("TRN2", target_bir_lowering=False, num_devices=1)
    aps = {k: nc.dram_tensor(f"in_{k}", v.shape, mybir.dt.from_np(v.dtype), kind="ExternalInput").ap()
           for k, v in arrays.items()}
    out = nc.dram_tensor("out_y", (128, 16, 256), F32, kind="ExternalOutput").ap()
    hybrid(nc, aps, out)
    r = run_bass_kernel_spmd(nc, [{f"in_{k}": v for k, v in arrays.items()}], core_ids=[0])
    y = r.results[0]["out_y"]
    return np.ascontiguousarray(y.transpose(2, 1, 0).reshape(1, 256, 2048))
```
